# Optimizing a Trainium2 kernel written in Bass

```python
import math
import jax, jax.numpy as jnp
from jax import lax
import numpy as np

D_MODEL = 1024
BATCH = 1
SEQ = 512
DEPTH = 2
DEC_BATCH = 8
DEC_SEQ = 1
PAST_LEN = 4096
PAGE_SIZE = 128

N_HEADS = 8
N_KV = 2
HPG = N_HEADS // N_KV
HEAD_DIM = 64
CMP_BLOCK = 32
CMP_STRIDE = 16
CMP_HIDDEN = 64
SEL_BLOCK = 64
N_SEL = 16
WINDOW = 512
QBLOCK = 64
D_A = D_MODEL // 4
CONV_A = 3
D_C = D_MODEL // 4
CONV_C = 31
N_BUCKETS = 32
MAX_DIST = 128
N_MEM = 256
X_HEADS = 4
X_HEAD_DIM = 128
D_FF = -(-8 * D_MODEL // (3 * 256)) * 256

Q_W = N_HEADS * HEAD_DIM
KV_W = 6 * N_KV * HEAD_DIM
NG_W = 3 * N_HEADS
A_W = 3 * D_A
C_W = 2 * D_C
MG_W = 3 * D_MODEL
P_IN = Q_W + KV_W + NG_W + A_W + C_W + MG_W
SPLITS = (Q_W, Q_W + KV_W, Q_W + KV_W + NG_W, Q_W + KV_W + NG_W + A_W, Q_W + KV_W + NG_W + A_W + C_W)

NEG_INF = -1e30
SEL_FORCE = 1e6
SEL_NEG = -1e9
RMS_EPS = 1e-6
LN_EPS = 1e-5

kernel_name = 'hybrid_nsa_shortconv_conformer_decoder_step'

def rms_norm(x, g):
    x32 = x.astype(jnp.float32)
    y = x32 * lax.rsqrt(jnp.mean(x32 * x32, axis=-1, keepdims=True) + RMS_EPS)
    return (y * g.astype(jnp.float32)).astype(x.dtype)

def layer_norm(x, g, b):
    x32 = x.astype(jnp.float32)
    mu = jnp.mean(x32, axis=-1, keepdims=True)
    xc = x32 - mu
    var = jnp.mean(xc * xc, axis=-1, keepdims=True)
    return (xc * lax.rsqrt(var + LN_EPS) * g.astype(jnp.float32) + b.astype(jnp.float32)).astype(x.dtype)

def rel_bucket(dist):
    n = jnp.maximum(dist, 0)
    exact = N_BUCKETS // 2
    large = exact + (jnp.log(jnp.maximum(n, exact).astype(jnp.float32) / exact)
                     / math.log(MAX_DIST / exact) * (N_BUCKETS - exact)).astype(jnp.int32)
    return jnp.where(n < exact, n, jnp.minimum(large, N_BUCKETS - 1))

def head_bias(rel_bias, dist):
    tq, nk = dist.shape
    b = rel_bias[rel_bucket(dist)].reshape(tq, nk, N_KV, HPG)
    return b.transpose(2, 3, 0, 1).astype(jnp.float32)

def masked_softmax(logits, mask):
    p = jax.nn.softmax(jnp.where(mask, logits.astype(jnp.float32), NEG_INF), axis=-1)
    return p * mask

def causal_dwconv(u, hist, w):
    width = w.shape[0]
    full = jnp.concatenate([hist, u], axis=1)
    y = lax.conv_general_dilated(full, w[:, None, :], window_strides=(1,), padding='VALID',
                                 dimension_numbers=('NWC', 'WIO', 'NWC'),
                                 feature_group_count=u.shape[-1])
    return y, full[:, -(width - 1):]

def compress_blocks(k, w1, b1, w2, b2, pe):
    B, L, G, D = k.shape
    nch = -(-L // CMP_STRIDE)
    k = jnp.pad(k, ((0, 0), (0, nch * CMP_STRIDE - L), (0, 0), (0, 0)))
    ch = k.reshape(B, nch, CMP_STRIDE, G, D).transpose(0, 1, 3, 2, 4).reshape(B, nch, G, CMP_STRIDE * D)
    half = CMP_STRIDE * D
    h = (jnp.einsum('bngf,fh->bngh', ch[:, :-1], w1[:half])
         + jnp.einsum('bngf,fh->bngh', ch[:, 1:], w1[half:])
         + (pe.reshape(-1) @ w1 + b1))
    return jnp.einsum('bngh,hd->bngd', jax.nn.silu(h), w2) + b2

def nsa_attention(q, k_cmp, v_cmp, k_sel, v_sel, k_win, v_win, gates, q_start, w_start,
                  rel_bias, cmp_w1, cmp_b1, cmp_w2, cmp_b2, cmp_pe, chunked):
    B, T = q.shape[:2]
    L = k_cmp.shape[1]
    scale = HEAD_DIM ** -0.5
    qg = q.reshape(B, T, N_KV, HPG, HEAD_DIM)
    qpos = q_start + jnp.arange(T, dtype=jnp.int32)

    ck = compress_blocks(k_cmp, cmp_w1[0], cmp_b1[0], cmp_w2[0], cmp_b2[0], cmp_pe[0])
    cv = compress_blocks(v_cmp, cmp_w1[1], cmp_b1[1], cmp_w2[1], cmp_b2[1], cmp_pe[1])
    nb = ck.shape[1]
    bend = jnp.arange(nb, dtype=jnp.int32) * CMP_STRIDE + (CMP_BLOCK - 1)
    dist_c = qpos[:, None] - bend[None, :]
    logits_c = jnp.einsum('btghd,bngd->bghtn', qg, ck).astype(jnp.float32) * scale + head_bias(rel_bias, dist_c)
    p_c = masked_softmax(logits_c, dist_c >= 0)
    o_c = jnp.einsum('bghtn,bngd->btghd', p_c.astype(cv.dtype), cv)

    ns = -(-L // SEL_BLOCK)
    cs = jnp.arange(nb, dtype=jnp.int32) * CMP_STRIDE
    ss = jnp.arange(ns, dtype=jnp.int32) * SEL_BLOCK
    overlap = ((cs[:, None] < ss[None, :] + SEL_BLOCK) & (cs[:, None] + CMP_BLOCK > ss[None, :])).astype(jnp.float32)
    p_s = jnp.einsum('bghtn,ns->bgts', p_c, overlap)
    jq = qpos // SEL_BLOCK
    jb = jnp.arange(ns, dtype=jnp.int32)
    future = jb[None, :] > jq[:, None]
    forced = (jb[None, :] == 0) | (jb[None, :] == jq[:, None]) | (jb[None, :] == jq[:, None] - 1)
    score = jnp.where(future, SEL_NEG, jnp.where(forced, SEL_FORCE, p_s))
    _, idx = lax.top_k(score, min(N_SEL, ns))

    pad = ns * SEL_BLOCK - L

    def to_blocks(a):
        a = jnp.pad(a, ((0, 0), (0, pad), (0, 0), (0, 0)))
        return a.reshape(B, ns, SEL_BLOCK, N_KV, HEAD_DIM).transpose(0, 3, 1, 2, 4)

    ksb, vsb = to_blocks(k_sel), to_blocks(v_sel)
    rb_g = rel_bias.reshape(N_BUCKETS, N_KV, HPG).transpose(1, 0, 2)
    bi = jnp.arange(B)[:, None, None, None]
    gi = jnp.arange(N_KV)[None, :, None, None]

    def local_branches(qc, ic, pc, kwc, vwc, kpc):
        kg = ksb[bi, gi, ic]
        vg = vsb[bi, gi, ic]
        spos = ic[..., None] * SEL_BLOCK + jnp.arange(SEL_BLOCK, dtype=jnp.int32)
        dist_s = pc[None, None, :, None, None] - spos
        bias_s = rb_g[gi[..., None], rel_bucket(dist_s)].transpose(0, 1, 5, 2, 3, 4).astype(jnp.float32)
        logit_s = jnp.einsum('btghd,bgtksd->bghtks', qc, kg).astype(jnp.float32) * scale + bias_s
        shp = logit_s.shape
        flat = shp[:4] + (shp[4] * shp[5],)
        mask_s = (dist_s >= 0).reshape(shp[0], shp[1], 1, shp[3], shp[4] * shp[5])
        p_sel = masked_softmax(logit_s.reshape(flat), mask_s).reshape(shp)
        o_s = jnp.einsum('bghtks,bgtksd->btghd', p_sel.astype(vg.dtype), vg)
        dist_w = pc[:, None] - kpc[None, :]
        mask_w = (dist_w >= 0) & (dist_w < WINDOW) & (kpc >= 0)[None, :]
        logit_w = jnp.einsum('btghd,blgd->bghtl', qc, kwc).astype(jnp.float32) * scale + head_bias(rel_bias, dist_w)
        p_w = masked_softmax(logit_w, mask_w)
        o_w = jnp.einsum('bghtl,blgd->btghd', p_w.astype(vwc.dtype), vwc)
        return o_s, o_w

    if chunked:
        n_chunks = T // QBLOCK
        kwp = jnp.pad(k_win, ((0, 0), (WINDOW, 0), (0, 0), (0, 0)))
        vwp = jnp.pad(v_win, ((0, 0), (WINDOW, 0), (0, 0), (0, 0)))

        def body(c):
            t0 = c * QBLOCK
            qc = lax.dynamic_slice_in_dim(qg, t0, QBLOCK, axis=1)
            ic = lax.dynamic_slice_in_dim(idx, t0, QBLOCK, axis=2)
            pc = q_start + t0 + jnp.arange(QBLOCK, dtype=jnp.int32)
            kwc = lax.dynamic_slice_in_dim(kwp, t0, WINDOW + QBLOCK, axis=1)
            vwc = lax.dynamic_slice_in_dim(vwp, t0, WINDOW + QBLOCK, axis=1)
            kpc = w_start + t0 - WINDOW + jnp.arange(WINDOW + QBLOCK, dtype=jnp.int32)
            return local_branches(qc, ic, pc, kwc, vwc, kpc)

        o_s, o_w = lax.map(body, jnp.arange(n_chunks, dtype=jnp.int32))
        o_s = jnp.moveaxis(o_s, 0, 1).reshape(B, T, N_KV, HPG, HEAD_DIM)
        o_w = jnp.moveaxis(o_w, 0, 1).reshape(B, T, N_KV, HPG, HEAD_DIM)
    else:
        kpc = w_start + jnp.arange(k_win.shape[1], dtype=jnp.int32)
        o_s, o_w = local_branches(qg, idx, qpos, k_win, v_win, kpc)

    g = gates.reshape(B, T, 3, N_KV, HPG)[..., None]
    o = g[:, :, 0] * o_c + g[:, :, 1] * o_s + g[:, :, 2] * o_w
    return o.reshape(B, T, N_HEADS * HEAD_DIM)

def mixer_block(h, lp, rel_bias, past):
    B, T, _ = h.shape
    z = h @ lp['w_in']
    q, kv, ng, a, c, mg = jnp.split(z, SPLITS, axis=-1)
    q = q.reshape(B, T, N_HEADS, HEAD_DIM)
    kv = kv.reshape(B, T, 6, N_KV, HEAD_DIM)
    kv_rows, win_rows = kv[:, :, :4], kv[:, :, 4:]
    if past is None:
        kv_all, win_all = kv_rows, win_rows
        q_start, w_start = 0, 0
        n_win = min(WINDOW, T)
        hist_a = jnp.zeros((B, CONV_A - 1, D_A), h.dtype)
        hist_c = jnp.zeros((B, CONV_C - 1, D_C), h.dtype)
        chunked = True
    else:
        kv_all = jnp.concatenate([past['kv'], kv_rows], axis=1)
        win_all = jnp.concatenate([past['win'], win_rows], axis=1)
        q_start = past['kv'].shape[1]
        n_win = past['win'].shape[1]
        w_start = q_start - n_win
        hist_a, hist_c = past['conv_a'], past['conv_c']
        chunked = False
    o_nsa = nsa_attention(q, kv_all[:, :, 0], kv_all[:, :, 1], kv_all[:, :, 2], kv_all[:, :, 3],
                          win_all[:, :, 0], win_all[:, :, 1],
                          jax.nn.sigmoid(ng.reshape(B, T, 3, N_HEADS)), q_start, w_start, rel_bias,
                          lp['cmp_w1'], lp['cmp_b1'], lp['cmp_w2'], lp['cmp_b2'], lp['cmp_pe'], chunked)
    a_in, a_b, a_c = jnp.split(a, 3, axis=-1)
    y_a, st_a = causal_dwconv(a_c * a_in, hist_a, lp['conv_a_w'])
    c_val, c_gate = jnp.split(c, 2, axis=-1)
    y_c, st_c = causal_dwconv(c_val * jax.nn.sigmoid(c_gate), hist_c, lp['conv_c_w'])
    y_c = jax.nn.silu(layer_norm(y_c + lp['conv_c_b'], lp['conv_c_ln_g'], lp['conv_c_ln_b']))
    gm = jax.nn.sigmoid(mg.reshape(B, T, 3, D_MODEL))
    merged = (gm[:, :, 0] * (o_nsa @ lp['w_nsa_out'])
              + gm[:, :, 1] * ((a_b * y_a) @ lp['w_a_out'])
              + gm[:, :, 2] * (y_c @ lp['w_c_out']))
    return merged @ lp['w_o'], (kv_rows, win_all[:, -n_win:], st_a, st_c)

def cross_attention(h, mem_kv, w_q, w_o):
    B, T, _ = h.shape
    q = (h @ w_q).reshape(B, T, X_HEADS, X_HEAD_DIM)
    logits = jnp.einsum('bthd,bmhd->bhtm', q, mem_kv[:, :, 0]).astype(jnp.float32) * (X_HEAD_DIM ** -0.5)
    p = jax.nn.softmax(logits, axis=-1).astype(mem_kv.dtype)
    o = jnp.einsum('bhtm,bmhd->bthd', p, mem_kv[:, :, 1]).reshape(B, T, X_HEADS * X_HEAD_DIM)
    return o @ w_o

def swiglu(h, w_up, w_down):
    g, u = jnp.split(h @ w_up, 2, axis=-1)
    return (jax.nn.silu(g) * u) @ w_down

def decoder_layer(x, mem_kv, past, lp, rel_bias):
    g = lp['norm_g']
    mix, st = mixer_block(rms_norm(x, g[0]), lp, rel_bias, past)
    x = x + rms_norm(mix, g[1])
    x = x + rms_norm(cross_attention(rms_norm(x, g[2]), mem_kv, lp['w_xq'], lp['w_xo']), g[3])
    x = x + rms_norm(swiglu(rms_norm(x, g[4]), lp['w_ffn_in'], lp['w_ffn_out']), g[5])
    return x, st

def setup_inputs(seed: int = 0) -> dict:
    key = jax.random.key(seed)
    ks = jax.random.split(key, 40)
    f32 = jnp.float32
    n_pages = PAST_LEN // PAGE_SIZE
    n_used = DEC_BATCH * n_pages
    n_pool = n_used + n_used // 4
    win_buf = min(WINDOW, PAST_LEN)

    def nrm(k, shape, scale=1.0):
        return jax.random.normal(k, shape, f32) * scale

    perm = jax.random.permutation(ks[5], n_pool)
    page_table = perm[:n_used].reshape(DEC_BATCH, n_pages).astype(jnp.int32)
    return {
        'x_prompt': nrm(ks[0], (BATCH, SEQ, D_MODEL)),
        'x_sample': nrm(ks[1], (DEC_BATCH, DEC_SEQ, D_MODEL)),
        'mem_prompt': nrm(ks[2], (BATCH, N_MEM, D_MODEL)),
        'cache_kv': nrm(ks[3], (DEPTH, n_pool, PAGE_SIZE, 4, N_KV, HEAD_DIM)),
        'page_table': page_table,
        'cache_win': nrm(ks[4], (DEPTH, DEC_BATCH, win_buf, 2, N_KV, HEAD_DIM)),
        'state_conv_a': nrm(ks[6], (DEPTH, DEC_BATCH, CONV_A - 1, D_A)),
        'state_conv_c': nrm(ks[7], (DEPTH, DEC_BATCH, CONV_C - 1, D_C)),
        'cache_mem': nrm(ks[8], (DEPTH, DEC_BATCH, N_MEM, 2, X_HEADS, X_HEAD_DIM)),
        'rel_bias': nrm(ks[9], (N_BUCKETS, N_HEADS), 0.5),
        'norm_g': 1.0 + nrm(ks[10], (DEPTH, 6, D_MODEL), 0.05),
        'mem_norm_g': 1.0 + nrm(ks[11], (DEPTH, D_MODEL), 0.05),
        'w_in': nrm(ks[12], (DEPTH, D_MODEL, P_IN), D_MODEL ** -0.5),
        'conv_a_w': nrm(ks[13], (DEPTH, CONV_A, D_A), CONV_A ** -0.5),
        'conv_c_w': nrm(ks[14], (DEPTH, CONV_C, D_C), CONV_C ** -0.5),
        'conv_c_b': nrm(ks[15], (DEPTH, D_C), 0.01),
        'conv_c_ln_g': 1.0 + nrm(ks[16], (DEPTH, D_C), 0.05),
        'conv_c_ln_b': nrm(ks[17], (DEPTH, D_C), 0.01),
        'cmp_w1': nrm(ks[18], (DEPTH, 2, CMP_BLOCK * HEAD_DIM, CMP_HIDDEN), (CMP_BLOCK * HEAD_DIM) ** -0.5),
        'cmp_b1': nrm(ks[19], (DEPTH, 2, CMP_HIDDEN), 0.01),
        'cmp_w2': nrm(ks[20], (DEPTH, 2, CMP_HIDDEN, HEAD_DIM), CMP_HIDDEN ** -0.5),
        'cmp_b2': nrm(ks[21], (DEPTH, 2, HEAD_DIM), 0.01),
        'cmp_pe': nrm(ks[22], (DEPTH, 2, CMP_BLOCK, HEAD_DIM), 0.1),
        'w_nsa_out': nrm(ks[23], (DEPTH, N_HEADS * HEAD_DIM, D_MODEL), (N_HEADS * HEAD_DIM) ** -0.5),
        'w_a_out': nrm(ks[24], (DEPTH, D_A, D_MODEL), D_A ** -0.5),
        'w_c_out': nrm(ks[25], (DEPTH, D_C, D_MODEL), D_C ** -0.5),
        'w_o': nrm(ks[26], (DEPTH, D_MODEL, D_MODEL), D_MODEL ** -0.5),
        'w_xq': nrm(ks[27], (DEPTH, D_MODEL, X_HEADS * X_HEAD_DIM), D_MODEL ** -0.5),
        'w_xkv': nrm(ks[28], (DEPTH, D_MODEL, 2 * X_HEADS * X_HEAD_DIM), D_MODEL ** -0.5),
        'w_xo': nrm(ks[29], (DEPTH, X_HEADS * X_HEAD_DIM, D_MODEL), (X_HEADS * X_HEAD_DIM) ** -0.5),
        'w_ffn_in': nrm(ks[30], (DEPTH, D_MODEL, 2 * D_FF), D_MODEL ** -0.5),
        'w_ffn_out': nrm(ks[31], (DEPTH, D_FF, D_MODEL), D_FF ** -0.5),
    }

def reference(x_prompt, x_sample, mem_prompt, cache_kv, page_table, cache_win, state_conv_a, state_conv_c,
              cache_mem, rel_bias, norm_g, mem_norm_g, w_in, conv_a_w, conv_c_w, conv_c_b, conv_c_ln_g,
              conv_c_ln_b, cmp_w1, cmp_b1, cmp_w2, cmp_b2, cmp_pe, w_nsa_out, w_a_out, w_c_out, w_o,
              w_xq, w_xkv, w_xo, w_ffn_in, w_ffn_out):
    n_seq_dec, n_pages = page_table.shape
    n_seq_p = mem_prompt.shape[0]
    yp, ys = x_prompt, x_sample
    kv_p, kv_s, win_p, win_s = [], [], [], []
    ca_p, ca_s, cc_p, cc_s, mem_p = [], [], [], [], []
    for l in range(DEPTH):
        lp = {
            'norm_g': norm_g[l], 'w_in': w_in[l],
            'conv_a_w': conv_a_w[l], 'conv_c_w': conv_c_w[l], 'conv_c_b': conv_c_b[l],
            'conv_c_ln_g': conv_c_ln_g[l], 'conv_c_ln_b': conv_c_ln_b[l],
            'cmp_w1': cmp_w1[l], 'cmp_b1': cmp_b1[l], 'cmp_w2': cmp_w2[l], 'cmp_b2': cmp_b2[l], 'cmp_pe': cmp_pe[l],
            'w_nsa_out': w_nsa_out[l], 'w_a_out': w_a_out[l], 'w_c_out': w_c_out[l], 'w_o': w_o[l],
            'w_xq': w_xq[l], 'w_xo': w_xo[l], 'w_ffn_in': w_ffn_in[l], 'w_ffn_out': w_ffn_out[l],
        }
        mkv_p = (rms_norm(mem_prompt, mem_norm_g[l]) @ w_xkv[l]).reshape(n_seq_p, N_MEM, 2, X_HEADS, X_HEAD_DIM)
        yp, stp = decoder_layer(yp, mkv_p, None, lp, rel_bias)
        past = {
            'kv': cache_kv[l][page_table].reshape(n_seq_dec, n_pages * PAGE_SIZE, 4, N_KV, HEAD_DIM),
            'win': cache_win[l], 'conv_a': state_conv_a[l], 'conv_c': state_conv_c[l],
        }
        ys, sts = decoder_layer(ys, cache_mem[l], past, lp, rel_bias)
        kv_p.append(stp[0]); win_p.append(stp[1]); ca_p.append(stp[2]); cc_p.append(stp[3])
        kv_s.append(sts[0]); win_s.append(sts[1]); ca_s.append(sts[2]); cc_s.append(sts[3])
        mem_p.append(mkv_p)
    return (yp, ys, jnp.stack(kv_p), jnp.stack(kv_s), jnp.stack(win_p), jnp.stack(win_s),
            jnp.stack(ca_p), jnp.stack(ca_s), jnp.stack(cc_p), jnp.stack(cc_s), jnp.stack(mem_p))


_drawn_inputs = setup_inputs


def setup_inputs(seed=0):
    import zlib

    import numpy as np

    out = dict(_drawn_inputs(seed))
    spreads = {}
    factors = {'conv_c_b': 4.868, 'conv_c_ln_b': 8.0, 'cmp_b1': 8.0, 'cmp_b2': 8.0}
    for name, (base, spread) in spreads.items():
        noise = np.random.default_rng([zlib.crc32(name.encode()), seed]).standard_normal(out[name].shape)
        drawn = base * np.exp(spread * noise) if base else spread * noise
        out[name] = __import__('jax').numpy.asarray(drawn.astype(out[name].dtype))
    for name, factor in factors.items():
        out[name] = (out[name] * factor).astype(out[name].dtype)
    return out
```

```python
from contextlib import ExitStack, contextmanager

import numpy as np

import concourse.bass as bass
from concourse import mybir

F32 = mybir.dt.float32
F32R = mybir.dt.float32r
I32 = mybir.dt.int32
U32 = mybir.dt.uint32
ALU = mybir.AluOpType
ACT = mybir.ActivationFunctionType
AX = mybir.AxisListType

P = 128
D_MODEL = 1024
KC = D_MODEL // P
SEQ = 512
NB = 8
TOK = SEQ + NB
HALF = TOK // 2
QT = SEQ // P
DEPTH = 2
PAST = 4096
PAGE = 128
POOL = 320
N_HEADS, N_KV, HD = 8, 2, 64
HPG = N_HEADS // N_KV
STRIDE, CMPB = 16, 32
SELB, N_SEL = 64, 16
WINDOW = 512
NBUCK = 32
N_MEM = 256
XH, XD = 4, 128
D_FF = 2816
FC = D_FF // P
CA, CC = 3, 31
Q_W, KV_W, NG_W, A_W, C_W = 512, 768, 24, 768, 512
COL_KV = Q_W
COL_NG = COL_KV + KV_W
COL_A = COL_NG + NG_W
COL_MG = COL_A + A_W + C_W
NEG = -1e30
V_GAIN, V_MEM, V_CA, V_CB, V_CG, V_CS, V_B1, V_B2, V_CC, V_PE, V_END = 0, 48, 56, 62, 64, 66, 68, 70, 72, 134, 166
RMS_EPS, LN_EPS = 1e-6, 1e-5
SEL_FORCE = 1e6

U_MIX, U_MG, U_OUT, U_WO, U_XKV, U_XQ, U_XO, U_FI, U_FO, U_END = 0, 20, 44, 52, 60, 68, 72, 80, 124, 148
RING = 4

BLK = 38
NEWS, WIN0, NEWW = 32, 33, 37
LINE = 640


def bucket(dist):
    n = np.maximum(dist, 0)
    exact = NBUCK // 2
    large = exact + (np.log(np.maximum(n, exact).astype(np.float32) / np.float32(exact))
                     / np.float32(np.log(128 / exact)) * np.float32(NBUCK - exact)).astype(np.int32)
    return np.where(n < exact, n, np.minimum(large, NBUCK - 1))


def onehot(dist):
    return (bucket(dist)[None] == np.arange(NBUCK).reshape((NBUCK,) + (1,) * dist.ndim)).astype(np.float32)


def shape_constants():
    p = np.arange(P)
    m = np.arange(LINE)
    line = onehot(np.maximum(SEQ - 1 - m, 0))
    dist = np.zeros((BLK, P), np.int64)
    for b in range(32):
        dist[b] = PAST - (STRIDE * (P * (b // 16) + p) + b % 16)
    for t in range(4):
        dist[WIN0 + t] = WINDOW - 4 * p - t
    cmp_dist = np.stack([PAST - (STRIDE * (P * t + p) + CMPB - 1) for t in range(2)])
    keys = onehot(np.concatenate([dist, cmp_dist]))
    n = np.arange(2 * P)
    s = np.arange(SELB + 1)
    ov = ((n[:, None] * STRIDE < s * SELB + SELB) & (n[:, None] * STRIDE + CMPB > s * SELB)).astype(np.float32)
    ov[2 * P - 1] = 0.0
    rt = (s[:, None] == n // 4).astype(np.float32)
    new = np.where(np.arange(NB)[:, None] == np.arange(NB), 0.0, NEG).astype(np.float32)
    kmask = np.zeros((P, 40), np.float32)
    kmask[0, WIN0] = NEG
    kmask[P - 1, 39] = NEG
    chunk = (p % 8).astype(np.float32).reshape(P, 1)
    return {"line": line, "keys": keys.reshape(NBUCK, 40 * P), "ov": ov.reshape(2, P, SELB + 1).transpose(1, 0, 2).copy(),
            "rt": rt, "new": new, "chunk": chunk, "kmask": kmask, "ident": np.eye(P, dtype=np.float32),
            "flip": np.ascontiguousarray(np.eye(P, dtype=np.float32)[::-1])}


class Chain:

    def __init__(self, done):
        self.done, self.n = done, 0

    def __call__(self, engine, instruction):
        self.n += 1
        instruction.then_inc(self.done, 1)
        engine.wait_ge(self.done, self.n)

    def restart(self, engine):
        engine.sem_clear(self.done)
        self.n = 0


def build(nc, A, O):
    stack = ExitStack()
    sems = []

    owner = [stack]

    def sem(name):
        s = owner[-1].enter_context(nc.semaphore(name))
        sems.append(s)
        return s

    @contextmanager
    def phase_semaphores():
        first = len(sems)
        with ExitStack() as scope:
            owner.append(scope)
            yield
            owner.pop()
            with nc.Block() as block:
                @block.gpsimd
                def _(e):
                    e.dma_reset()
                    for s in sems[first:]:
                        e.sem_clear(s)
            del sems[first:]

    def sb(scope, name, shape, dt=F32):
        return scope.enter_context(nc.sbuf_tensor(name, shape, dt))

    def await_reg(e, s, value):
        e.wait_ge(s, value)
        e.sem_inc(passed, 1)

    with stack:
        xT = sb(stack, "xT", [P, KC, TOK])
        act_hi = sb(stack, "act_hi", [P, KC, TOK], F32R)
        act_lo = sb(stack, "act_lo", [P, KC, TOK], F32R)
        w_raw = sb(stack, "w_raw", [P, RING, KC * P])
        w_hi = sb(stack, "w_hi", [P, 2, KC * P], F32R)
        w_lo = sb(stack, "w_lo", [P, 2, KC * P], F32R)
        ident = sb(stack, "ident", [P, P])
        ones = sb(stack, "ones", [P, P])
        ov = sb(stack, "ov", [P, 2, SELB + 1])
        rt = sb(stack, "rt", [SELB + 1, 2 * P])
        key_bias = sb(stack, "key_bias", [P, 40, N_HEADS])
        new_bias = sb(stack, "new_bias", [NB, NB, N_HEADS])
        gather_rows = sb(stack, "gather_rows", [P, NB * 8], U32)
        vecs = sb(stack, "vecs", [P, V_END])
        minus_half = sb(stack, "minus_half", [P, NB])
        pg = stack.enter_context(nc.psum_tensor("pg", [P, 2, 2, 512], F32))
        pn = stack.enter_context(nc.psum_tensor("pn", [P, 2, 512], F32))
        pa = [stack.enter_context(nc.psum_tensor(f"pa{i}", [P, 512], F32)) for i in range(2)]
        line_dram = nc.dram_tensor("line_scratch", [N_HEADS, LINE], F32)
        toep_dram = nc.dram_tensor("toep_scratch", [N_HEADS, P, SEQ], F32)
        mem_dram = nc.dram_tensor("mem_scratch", [P, KC * N_MEM], F32)

        passed = sem("passed")
        dve_chain, act_chain, pool_chain = Chain(sem("dve_done")), Chain(sem("act_done")), Chain(sem("pool_done"))
        raw_full = [sem(f"raw_full{i}") for i in range(RING)]
        whi_ready, w_ready = sem("whi_ready"), sem("w_ready")
        unit_done = sem("unit_done")
        evac = [sem("evac0"), sem("evac1")]
        sq_ready, sq_used, ms_ready, rstd_ready = (sem(n) for n in ("sq_ready", "sq_used", "ms_ready", "rstd_ready"))
        diag_ready, rstd_bc, t_ready, hi_ready, even_ended, odd_ended = (sem(n) for n in (
            "diag_ready", "rstd_bc", "t_ready", "hi_ready", "even_ended", "odd_ended"))

        C = {k: nc.inline_tensor(v, "c_" + k) for k, v in shape_constants().items()}

        def halves(ap):
            return ap.rearrange("p (h c) -> p h c", h=2)

        with phase_semaphores(), ExitStack() as scope:
            x_nat = sb(scope, "x_nat", [P, 5, D_MODEL])
            m_nat = sb(scope, "m_nat", [P, 2, D_MODEL])
            m_sq = sb(scope, "m_sq", [P, D_MODEL])
            m_ms = sb(scope, "m_ms", [P, 2])
            m_rstd = sb(scope, "m_rstd", [P, 2])
            memT = sb(scope, "memT", [P, KC, N_MEM])
            keys = sb(scope, "keys", [NBUCK, 40 * P])
            line1h = sb(scope, "line1h", [NBUCK, LINE])
            rel = sb(scope, "rel", [NBUCK, N_HEADS])
            line = sb(scope, "line", [N_HEADS, LINE])
            new = sb(scope, "new", [NB, NB])
            kmask = sb(scope, "kmask", [P, 40])
            pages = sb(scope, "pages", [P, NB, 2], I32)
            pagef = sb(scope, "pagef", [P, NB, 2])
            rowf = sb(scope, "rowf", [P, NB, 2])
            chunk = sb(scope, "chunk", [P, 1])
            flip = sb(scope, "flip", [P, P])
            toep_up = sb(scope, "toep_up", [P, N_HEADS, SEQ])
            toep = sb(scope, "toep", [P, N_HEADS, SEQ])
            toep_in, flip_done, flip_used = (sem(n) for n in ("toep_in", "flip_done", "flip_used"))
            ld, ldx, ldp, line_out, setup_out = (sem(n) for n in ("ld", "ldx", "ldp", "line_out", "setup_out"))
            tr_done, tr_used, m_sqs, m_pow = (sem(n) for n in ("tr_done", "tr_used", "m_sqs", "m_pow"))
            mem_scaled, line_ready, keys_done, line_mm, fill = (sem(n) for n in ("mem_scaled", "line_ready", "keys_done", "line_mm", "fill"))
            NLD = 10
            with nc.Block() as block:
                @block.sync
                def _(e):
                    e.dma_start(x_nat[:, 0:4, :], A["x_prompt"].rearrange("o (t p) d -> p (o t) d", p=P)).then_inc(ldx, 16)
                    e.dma_start(x_nat[0:NB, 4, :], A["x_sample"].rearrange("b o d -> (b o) d")).then_inc(ldx, 16)
                    e.dma_start(m_nat[:], A["mem_prompt"].rearrange("o (t p) d -> p (o t) d", p=P)).then_inc(ldx, 16)
                    for dst, src in ((ident[:], C["ident"]), (keys[:], C["keys"]), (line1h[:], C["line"]), (new[:], C["new"]),
                                     (ov[:], C["ov"]), (rt[:], C["rt"]), (chunk[:], C["chunk"]), (kmask[:], C["kmask"]), (flip[:], C["flip"])):
                        e.dma_start(dst, src.ap()).then_inc(ld, 16)
                    e.dma_start(rel[:], A["rel_bias"]).then_inc(ld, 16)
                    e.wait_ge(line_ready, 2)
                    e.dma_start(line_dram.ap(), line[:]).then_inc(line_out, 16)
                    e.wait_ge(line_out, 16)
                    src = bass.AP(line_dram.ap().tensor, 0, [[1, P], [LINE, N_HEADS], [1, SEQ]])
                    e.dma_start(toep_up[:], src).then_inc(toep_in, 16)
                    e.wait_ge(flip_used, N_HEADS)
                    e.dma_start(toep_dram.ap().rearrange("h p q -> p h q"), toep[:]).then_inc(setup_out, 16)
                    e.wait_ge(tr_used, 14)
                    e.dma_start(mem_dram.ap(), memT[:].rearrange("p c m -> p (c m)")).then_inc(setup_out, 16)
                    e.wait_ge(setup_out, 32)

                @block.gpsimd
                def _(e):
                    for a in range(16):
                        e.dma_start(pages[8 * a:8 * a + 8, :, :],
                                    A["page_table"].rearrange("b (t a) -> a b t", a=16)[a:a + 1].broadcast_to([8, NB, 2]), allow_slow_non_contiguous=True
                                    ).then_inc(ldp, 16)
                    e.wait_ge(ldp, 256)
                    e.memset(minus_half[:], -0.5).then_inc(fill, 1)
                    e.wait_ge(fill, 1)
                    e.wait_ge(m_sqs, 3)
                    e.tensor_tensor(m_rstd[:], m_ms[:], minus_half[:, 0:2], ALU.pow).then_inc(m_pow, 1)

                @block.scalar
                def _(e):
                    e.wait_ge(ldx, 48)
                    for t in range(2):
                        if t:
                            e.wait_ge(m_sqs, 1)
                        e.activation(m_sq[:], m_nat[:, t, :], ACT.Square, accum_out=m_ms[:, t:t + 1]).then_inc(m_sqs, 1)

                @block.vector
                def _(e):
                    link = lambda i: dve_chain(e, i)
                    link(e.memset(ones[:], 1.0))
                    e.wait_ge(m_sqs, 2)
                    e.tensor_scalar(m_ms[:], m_ms[:], 1.0 / D_MODEL, RMS_EPS, ALU.mult, ALU.add).then_inc(m_sqs, 1)
                    e.wait_ge(ldp, 256)
                    e.wait_ge(ld, 16 * NLD)
                    link(e.tensor_copy(pagef[:], pages[:]))
                    link(e.scalar_tensor_tensor(rowf[:], pagef[:], 8.0, chunk[:, 0:1].rearrange("p (a b) -> p a b", a=1).broadcast_to([P, NB, 2]), ALU.mult, ALU.add))
                    rows = gather_rows[:].rearrange("p (b t q) -> p b t q", t=2, q=4)
                    for q in range(4):
                        link(e.tensor_scalar(rows[:, :, :, q], rowf[:], 4.0, float(q), ALU.mult, ALU.add))
                    e.wait_ge(line_mm, 1)
                    e.tensor_copy(line[:, 0:512], pn[0:N_HEADS, 0, :]).then_inc(line_ready, 1)
                    e.memset(line[:, 512:LINE], NEG).then_inc(line_ready, 1)
                    e.wait_ge(keys_done, 1)
                    link(e.tensor_tensor(key_bias[:], pg[:, 0, 0, 0:320].rearrange("p (b h) -> p b h", h=N_HEADS),
                                         kmask[:].rearrange("p (b o) -> p b o", o=1).broadcast_to([P, 40, N_HEADS]), ALU.add))
                    link(e.tensor_tensor(new_bias[:], new[:].rearrange("p (b o) -> p b o", o=1).broadcast_to([NB, NB, N_HEADS]),
                                         key_bias[0:NB, NEWS:NEWS + 1, :].broadcast_to([NB, NB, N_HEADS]), ALU.add))
                    e.wait_ge(m_pow, 1)
                    for t in range(2):
                        e.tensor_scalar(m_nat[:, t, :], m_nat[:, t, :], m_rstd[:, t:t + 1], None, ALU.mult).then_inc(mem_scaled, 1)
                    n = 0
                    for t in range(5):
                        w = P if t < 4 else NB
                        for q in range(2):
                            e.wait_ge(tr_done, n + 1)
                            src = pa[n % 2][:].rearrange("p (c w) -> p c w", c=4)[:, :, 0:w]
                            e.tensor_copy(xT[:, 4 * q:4 * q + 4, P * t:P * t + w], src).then_inc(tr_used, 1)
                            n += 1
                    for t in range(2):
                        for q in range(2):
                            e.wait_ge(tr_done, n + 1)
                            e.tensor_copy(memT[:, 4 * q:4 * q + 4, P * t:P * t + P],
                                          pa[n % 2][:].rearrange("p (c w) -> p c w", c=4)).then_inc(tr_used, 1)
                            n += 1
                    for h in range(N_HEADS):
                        e.wait_ge(flip_done, h + 1)
                        e.tensor_copy(toep[:, h, :], pg[:, 1, h % 2, :]).then_inc(flip_used, 1)

                @block.tensor
                def _(e):
                    e.wait_ge(ld, 16 * NLD)
                    e.matmul(pn[0:N_HEADS, 0, :], rel[:], line1h[:, 0:512], start=True, stop=True).then_inc(line_mm, 1)
                    for b in range(40):
                        mm = e.matmul(pg[:, 0, 0, b * N_HEADS:(b + 1) * N_HEADS], keys[:, b * P:(b + 1) * P], rel[:],
                                      start=True, stop=True)
                    mm.then_inc(keys_done, 1)
                    e.wait_ge(ldx, 48)
                    n = 0
                    for t in range(7):
                        w = NB if t == 4 else P
                        src = x_nat if t < 5 else m_nat
                        if t >= 5:
                            e.wait_ge(mem_scaled, t - 4)
                        for q in range(2):
                            if n >= 2:
                                e.wait_ge(tr_used, n - 1)
                            for c in range(4):
                                mm = e.transpose(pa[n % 2][:, c * P:c * P + w], src[0:w, t if t < 5 else t - 5, (4 * q + c) * P:(4 * q + c + 1) * P],
                                                 ident[0:w, 0:w])
                            mm.then_inc(tr_done, 1)
                            n += 1
                    e.wait_ge(toep_in, 16)
                    for h in range(N_HEADS):
                        if h >= 2:
                            e.wait_ge(flip_used, h - 1)
                        e.matmul(pg[:, 1, h % 2, :], flip[:], toep_up[:, h, :], start=True, stop=True).then_inc(flip_done, 1)

        def fori(e, lo, hi, body):
            if hi - lo == 1:
                body(lo)
            elif hi > lo:
                with e.Fori(lo, hi) as j:
                    body(j)

        def await_(e, s, value):
            if isinstance(value, int):
                if value > 0:
                    e.wait_ge(s, value)
            else:
                await_reg(e, s, value)

        def copies(u):
            return 2 if u < 4 else 4 if U_OUT <= u < U_WO else 1

        def landed(u):
            return 16 * sum(copies(v) for v in range(u % RING, u + 1, RING))

        def landed_at(u, lo, j):
            return landed(u) + 16 * copies(u) * (j - lo)

        def load_unit(e, u, slot, parts, free):
            if free is not None:
                await_(e, w_ready, free)
            for dst, src in parts:
                e.dma_start(dst, src).then_inc(raw_full[slot], 16)

        def slot_view(slot):
            return w_raw[:, slot, :].rearrange("p (k n) -> p k n", n=P)

        def split_hi(e, v, slot, full):
            await_(e, raw_full[slot], full)
            await_(e, unit_done, v - 1)
            e.copy(w_hi[:, slot % 2, :], w_raw[:, slot, :]).then_inc(whi_ready, 1)

        def split_lo(e, v, slot):
            await_(e, whi_ready, v + 1)
            e.tensor_tensor(w_lo[:, slot % 2, :], w_raw[:, slot, :], w_hi[:, slot % 2, :].bitcast(F32),
                            ALU.subtract).then_inc(w_ready, 1)

        def unit_groups(e, u0, n, split, step, lo=0, unroll=False):
            last = n // RING - 1

            def group(j):
                for s in range(RING):
                    ahead = u0 + RING * lo + s + 1
                    if isinstance(j, int):
                        ahead = u0 + RING * j + s + 1
                        if ahead < U_END:
                            split(ahead, (s + 1) % RING, landed(ahead))
                    else:
                        split(u0 + RING * j + s + 1, (s + 1) % RING, landed_at(ahead, lo, j))
                    step(j, s)
            if unroll:
                for j in range(lo, last):
                    group(j)
            elif last > lo:
                fori(e, lo, last, group)
            group(last)

        def products(e, v, slot, tile, tslot, k0, kn, operand, first, last, widths):
            await_(e, w_ready, v + 1)
            if first:
                await_(e, evac[tslot], tile)
            hi, lo = operand
            for k in range(kn):
                wk = slice(k * P, (k + 1) * P)
                trio = ((w_lo, hi), (w_hi, lo), (w_hi, hi))
                for n, (w, x) in enumerate(trio):
                    at = 0
                    for h, wd in enumerate(widths):
                        mm = e.matmul(pg[:, tslot, h, 0:wd], w[:, slot % 2, wk], x[:, k0 + k, at:at + wd],
                                      start=first and k == 0 and n == 0, stop=last and k == kn - 1 and n == 2)
                        at += wd
            mm.then_inc(unit_done, 1)

        def plain_stage(e, u0, n, operand, kn=KC, widths=(HALF, HALF), lo=0):
            def group(j):
                for s in range(RING):
                    u = u0 + RING * j + s
                    products(e, u, s, u0 // 2 + 2 * j + s // 2, s % 2, 0, kn, operand, True, True, widths)
            if u0 == 0 and lo == 0:
                group(0)
                lo = 1
            fori(e, lo, n // RING, group)

        def weights(e, u0, n, parts, lo=0):
            def group(j):
                for s in range(RING):
                    u = u0 + RING * j + s
                    free = None if isinstance(u, int) and u < RING else u - RING + 1
                    load_unit(e, u, s, parts(j, s), free)
            fori(e, lo, n // RING, group)

        def tile_done_(e, u):
            await_(e, unit_done, u + 1)

        def out_tile(tslot, w=HALF):
            return pg[:, tslot, :, 0:w]

        def norm_block(*norms):
            with ExitStack() as scope:
                tag = norms[0][0]
                sq = sb(scope, f"sq{tag}", [P, 2, TOK])
                t = sb(scope, f"t{tag}", [P, 2, TOK])
                ms = sb(scope, f"ms{tag}", [P, NB])
                r = sb(scope, f"r{tag}", [P, NB])
                diag = sb(scope, f"diag{tag}", [P, TOK])
                ended = (even_ended, odd_ended)
                HC = KC // 2

                def end_chunk(e, k, c, pre):
                    if pre:
                        e.wait_ge(hi_ready, KC * (k // 2) + c + 1)
                        mm = e.tensor_tensor(act_lo[:, c, :], t[:, c % 2, :], act_hi[:, c, :].bitcast(F32), ALU.subtract)
                    else:
                        e.wait_ge(t_ready, KC * k + c + 1)
                        mm = e.tensor_tensor(xT[:, c, :], xT[:, c, :], t[:, c % 2, :], ALU.add)
                    mm.then_inc(ended[c % 2], 1)

                with nc.Block() as block:
                    @block.scalar
                    def _(e):
                        for i, (k, x, pre) in enumerate(norms):
                            for c in range(KC):
                                if i:
                                    e.wait_ge(ended[c % 2], HC * (k - 1) + c // 2 + 1)
                                if i or c >= 2:
                                    e.wait_ge(sq_used, KC * k + c - 1)
                                e.activation(sq[:, c % 2, :], x[:, c, :], ACT.Square).then_inc(sq_ready, 1)
                            if pre:
                                for c in range(KC):
                                    e.wait_ge(t_ready, KC * k + c + 1)
                                    e.copy(act_hi[:, c, :], t[:, c % 2, :]).then_inc(hi_ready, 1)

                    @block.tensor
                    def _(e):
                        for i, (k, x, pre) in enumerate(norms):
                            for c in range(KC):
                                e.wait_ge(sq_ready, KC * k + c + 1)
                                for tt in range(5):
                                    w = P if tt < 4 else NB
                                    mm = e.matmul(pa[i][0:w, tt:tt + 1], sq[:, c % 2, tt * P:tt * P + w], ones[:, 0:1],
                                                  start=c == 0 and tt == 0, stop=c == KC - 1, skip_group_check=True)
                                mm.then_inc(sq_used, 1)
                            e.wait_ge(diag_ready, k + 1)
                            for h in range(2):
                                mm = e.matmul(pn[:, h, 0:HALF], ones[:], diag[:, h * HALF:(h + 1) * HALF], start=True, stop=True)
                            mm.then_inc(rstd_bc, 1)

                    @block.gpsimd
                    def _(e):
                        for k, x, pre in norms:
                            e.wait_ge(ms_ready, k + 1)
                            e.tensor_tensor(r[:], ms[:], minus_half[:], ALU.pow).then_inc(rstd_ready, 1)
                            for c in range(1, KC, 2):
                                end_chunk(e, k, c, pre)

                    @block.vector
                    def _(e):
                        link = lambda i: dve_chain(e, i)
                        link(e.memset(ms[:], 1.0))
                        for i, (k, x, pre) in enumerate(norms):
                            e.wait_ge(sq_used, KC * (k + 1))
                            link(e.tensor_scalar(ms[:, 0:4], pa[i][:, 0:4], 1.0 / D_MODEL, RMS_EPS, ALU.mult, ALU.add))
                            e.tensor_scalar(ms[0:NB, 4:5], pa[i][0:NB, 4:5], 1.0 / D_MODEL, RMS_EPS, ALU.mult, ALU.add
                                            ).then_inc(ms_ready, 1)
                            e.wait_ge(rstd_ready, k + 1)
                            link(e.tensor_tensor(diag[:, 0:SEQ].rearrange("p (t q) -> p t q", t=4),
                                                 ident[:].rearrange("p (o q) -> p o q", o=1).broadcast_to([P, 4, P]),
                                                 r[:, 0:4].rearrange("p (t o) -> p t o", o=1).broadcast_to([P, 4, P]), ALU.mult))
                            e.tensor_scalar(diag[:, SEQ:TOK], ident[:, 0:NB], r[:, 4:5], None, ALU.mult).then_inc(diag_ready, 1)
                            e.wait_ge(rstd_bc, k + 1)
                            for c in range(KC):
                                if c >= 2:
                                    e.wait_ge(ended[c % 2], HC * k + c // 2)
                                elif i:
                                    e.wait_ge(ended[c], HC * k)
                                e.scalar_tensor_tensor(halves(t[:, c % 2, :]), halves(x[:, c, :]), vecs[:, V_GAIN + KC * k + c:V_GAIN + KC * k + c + 1],
                                                       pn[:, :, 0:HALF], ALU.mult, ALU.mult).then_inc(t_ready, 1)
                                if c % 2:
                                    end_chunk(e, k, c - 1, pre)

        def semaphores_to_zero():
            with nc.Block() as block:
                @block.gpsimd
                def _(e):
                    e.dma_reset()
                    for s in sems:
                        e.sem_clear(s)
            for c in (dve_chain, act_chain, pool_chain):
                c.n = 0

        semaphores_to_zero()
        with nc.Fori(0, DEPTH) as L:
            def at_layer(name):
                return A[name][bass.ds(L, 1)]

            def cols(name, start, rows=slice(0, D_MODEL)):
                m = at_layer(name)[:, rows, bass.ds(start, P)]
                return m.rearrange("o (k p) n -> p (o k) n", p=P)

            def mix_parts(j, s):
                dst = slot_view(s)
                if isinstance(j, int) and j == 0:
                    return [(dst[:, :, g * HD:(g + 1) * HD],
                             at_layer("w_in")[:, :, (g * HPG + s) * HD:(g * HPG + s + 1) * HD].rearrange("o (k p) n -> p (o k) n", p=P))
                            for g in range(2)]
                t = RING * (j - 1) + s
                return [(dst, cols("w_in", COL_KV + P * t + (NG_W if t >= 6 else 0)))]

            def std_parts(name, base=0):
                def parts(j, s):
                    return [(slot_view(s), cols(name, base + P * s + j * (RING * P)))]
                return parts

            def out_parts(j, s):
                v = slot_view(s)
                col = bass.ds(P * s + j * (RING * P), P)
                nsa = at_layer("w_nsa_out")
                return [(v[g * HD:(g + 1) * HD, 0:4, :], nsa[:, g * 256:(g + 1) * 256, col].rearrange("o (k p) n -> p (o k) n", p=HD))
                        for g in range(2)] + [
                    (v[:, 4 + 2 * i:6 + 2 * i, :], at_layer(nm)[:, :, col].rearrange("o (k p) n -> p (o k) n", p=P))
                    for i, nm in enumerate(("w_a_out", "w_c_out"))]

            def fi_parts(j, s):
                return [(slot_view(s), cols("w_ffn_in", (s % 2) * D_FF + P * (s // 2) + j * (2 * P)))]

            def xo_parts(j, s):
                return [(slot_view(s)[:, 0:XH, :], cols("w_xo", P * s + j * (RING * P), slice(0, XH * XD)))]

            upto_b3 = ExitStack()
            upto_b4 = ExitStack()
            oac = sb(upto_b4, "oac", [P, 6, TOK])
            u_c = sb(upto_b4, "u_c", [P, 2, CC - 1 + TOK])
            us_c = sb(upto_b4, "us_c", [P, 2, CC, NB])
            w1 = sb(upto_b3, "w1", [P, 2, 8, P])
            w2 = sb(upto_b3, "w2", [P, 2, P])
            b2row = sb(upto_b3, "b2row", [P, P])
            cbias = sb(upto_b3, "cbias", [P, 2])
            gateT = sb(upto_b3, "gateT", [NG_W, TOK])
            k_new = sb(upto_b3, "k_new", [P, 2, NB])
            nat_new = sb(upto_b3, "nat_new", [NB, KV_W])
            q_blk = sb(upto_b3, "q_blk", [P, NB, N_HEADS])

            with ExitStack() as scope:
                rows_a = sb(scope, "rows_a", [72, P])
                rows_b = sb(scope, "rows_b", [62, P])
                rows_pe = sb(scope, "rows_pe", [32, P])
                vl, w1l, w2l, w2z, vt, vdone, pem, cbs = (sem(n) for n in ("vl", "w1l", "w2l", "w2z", "vt", "vdone", "pem", "cbs"))
                with nc.Block() as block:
                    @block.sync
                    def _(e):
                        vec = [("norm_g", 0, 48, "o k (c p) -> (o k c) p"), ("mem_norm_g", 48, 8, "o (c p) -> (o c) p"),
                               ("conv_a_w", 56, 6, "o k (c p) -> (o k c) p"), ("conv_c_b", 62, 2, "o (c p) -> (o c) p"),
                               ("conv_c_ln_g", 64, 2, "o (c p) -> (o c) p"), ("conv_c_ln_b", 66, 2, "o (c p) -> (o c) p")]
                        for name, at, n, how in vec:
                            e.dma_start(rows_a[at:at + n, :], at_layer(name).rearrange(how, p=P)).then_inc(vl, 16)
                        for at, name in ((68, "cmp_b1"), (70, "cmp_b2")):
                            for g in range(2):
                                e.dma_start(rows_a[at:at + 2, g * 64:(g + 1) * 64], at_layer(name).rearrange("o k h -> (o k) h")).then_inc(vl, 16)
                        e.dma_start(rows_b[:], at_layer("conv_c_w").rearrange("o k (c p) -> (o k c) p", p=P)).then_inc(vl, 16)
                        e.dma_start(rows_pe[:], at_layer("cmp_pe").rearrange("o k (t q) d -> (o k t) (q d)", q=2)).then_inc(vl, 16)
                        for kv in range(2):
                            for half in range(2):
                                src = A["cmp_w1"][bass.ds(L, 1), kv:kv + 1, half * 1024:(half + 1) * 1024, :]
                                e.dma_start(w1[:, kv, :, half * 64:(half + 1) * 64], src.rearrange("o x (i q) h -> q (o x i) h", q=P)).then_inc(w1l, 16)
                        e.wait_ge(w2z, 1)
                        for kv in range(2):
                            for g in range(2):
                                src = A["cmp_w2"][bass.ds(L, 1), kv:kv + 1].rearrange("o x h d -> (o x h) d")
                                e.dma_start(w2[g * 64:(g + 1) * 64, kv, g * 64:(g + 1) * 64], src).then_inc(w2l, 16)
                        for g in range(2):
                            src = A["cmp_b2"][bass.ds(L, 1), 1:2].rearrange("o x d -> (o x) d").broadcast_to([P, HD])
                            e.dma_start(b2row[:, g * 64:(g + 1) * 64], src).then_inc(w2l, 16)
                        weights(e, U_MIX, RING, mix_parts)

                    @block.gpsimd
                    def _(e):
                        e.memset(w2[:], 0.0).then_inc(w2z, 1)

                    @block.tensor
                    def _(e):
                        e.wait_ge(vl, 192)
                        e.transpose(pa[0][:, 0:72], rows_a[:], ident[0:72, 0:72])
                        e.transpose(pa[0][:, 72:134], rows_b[:], ident[0:62, 0:62])
                        e.transpose(pa[0][:, 134:166], rows_pe[:], ident[0:32, 0:32]).then_inc(vt, 1)

                    @block.vector
                    def _(e):
                        e.wait_ge(vt, 1)
                        e.tensor_copy(vecs[:], pa[0][:, 0:V_END]).then_inc(vdone, 1)

            norm_block((0, xT, True))
            upto_b2 = ExitStack()
            z = sb(upto_b2, "z", [P, 20, TOK])
            Z_K, Z_A, Z_C = 4, 10, 16
            with ExitStack() as scope:
                ng_raw = sb(scope, "ng_raw", [P, KC * P])
                ng_hi = sb(scope, "ng_hi", [P, KC * P], F32R)
                ng_lo = sb(scope, "ng_lo", [P, KC * P], F32R)
                th = sb(scope, "th", [NG_W, TOK])
                ng_l, ng_h, ng_r, ng_mm, ng_th = (sem(n) for n in ("ng_l", "ng_h", "ng_r", "ng_mm", "ng_th"))
                with nc.Block() as block:
                    @block.sync
                    def _(e):
                        for j in range(1, 5):
                            for s in range(RING):
                                load_unit(e, RING * j + s, s, mix_parts(j, s), RING * j + s - RING + 1)
                        e.dma_start(ng_raw[:].rearrange("p (k n) -> p k n", n=P), cols("w_in", COL_NG)).then_inc(ng_l, 16)
                        load_unit(e, U_MG, 0, std_parts("w_in", COL_MG)(0, 0), U_MG - RING + 1)

                    @block.scalar
                    def _(e):
                        def step(j, s):
                            u = RING * j + s
                            tile_done_(e, u)
                            e.copy(halves(z[:, bass.ds(u, 1), :].rearrange("p o t -> p (o t)")), out_tile(s % 2)).then_inc(evac[s % 2], 1)
                        split = lambda v, slot, full: split_hi(e, v, slot, full)
                        e.wait_ge(raw_full[0], landed(0))
                        e.copy(w_hi[:, 0, :], w_raw[:, 0, :]).then_inc(whi_ready, 1)
                        for s in range(RING):
                            if s == 0:
                                e.wait_ge(raw_full[1], landed(1))
                                e.copy(w_hi[:, 1, :], w_raw[:, 1, :]).then_inc(whi_ready, 1)
                            else:
                                split(s + 1, (s + 1) % RING, landed(s + 1))
                            step(0, s)
                        unit_groups(e, U_MIX, 20, split, step, lo=1)
                        e.wait_ge(ng_l, 16)
                        e.copy(ng_hi[:], ng_raw[:]).then_inc(ng_h, 1)
                        e.wait_ge(ng_mm, 1)
                        e.activation(halves(th[:]), pn[0:NG_W, :, 0:HALF], ACT.Tanh, scale=0.5).then_inc(ng_th, 1)

                    @block.vector
                    def _(e):
                        split = lambda v, slot, full: split_lo(e, v, slot)
                        split(0, 0, None)
                        for s in range(RING):
                            split(s + 1, (s + 1) % RING, None)
                        unit_groups(e, U_MIX, 20, split, lambda j, s: None, lo=1)
                        e.wait_ge(ng_h, 1)
                        e.tensor_tensor(ng_lo[:], ng_raw[:], ng_hi[:].bitcast(F32), ALU.subtract).then_inc(ng_r, 1)
                        e.wait_ge(ng_th, 1)
                        e.tensor_scalar(gateT[:], th[:], 0.5, 0.5, ALU.mult, ALU.add)

                    @block.tensor
                    def _(e):
                        plain_stage(e, U_MIX, 20, (act_hi, act_lo))
                        e.wait_ge(ng_r, 1)
                        for k in range(KC):
                            wk = slice(k * P, (k + 1) * P)
                            for n, (w, x) in enumerate(((ng_lo, act_hi), (ng_hi, act_lo), (ng_hi, act_hi))):
                                for h in range(2):
                                    mm = e.matmul(pn[:, h, 0:HALF], w[:, wk], x[:, k, h * HALF:(h + 1) * HALF],
                                                  start=k == 0 and n == 0, stop=k == KC - 1 and n == 2)
                        mm.then_inc(ng_mm, 1)

            nat = sb(upto_b2, "nat", [P, 5, KV_W])
            ends = sb(upto_b2, "ends", [38, 2, 2 * P])
            gate_n = sb(upto_b2, "gate_n", [P, QT, NG_W])
            with ExitStack() as scope:
                u_a = sb(scope, "u_a", [P, 2, CA - 1 + TOK])
                us_a = sb(scope, "us_a", [P, 2, CA, NB])
                th = sb(scope, "thc", [P, 2, TOK])
                y_a = sb(scope, "y_a", [P, 2, TOK])
                st_a = sb(scope, "st_a", [NB * (CA - 1), 2 * P])
                st_c = sb(scope, "st_c", [120, 2, 2 * P])
                cb = sb(scope, "cb", [64, 4])
                st_l, nt_done, nt_used, tanh_c, ua_ready, uc_ready = (sem(n) for n in ("st_l", "nt_done", "nt_used", "tanh_c", "ua_ready", "uc_ready"))
                st_tr, end_tr, end_ready, outs = (sem(n) for n in ("st_tr", "end_tr", "end_ready", "outs"))
                with nc.Block() as block:
                    @block.sync
                    def _(e):
                        e.dma_start(st_a[:], at_layer("state_conv_a").rearrange("o b t d -> (o b t) d")).then_inc(st_l, 16)
                        e.dma_start(st_c[:], at_layer("state_conv_c").rearrange("o (q b) t d -> (b t) (o q) d", q=2)).then_inc(st_l, 16)
                        o_layer = lambda n: O[n][bass.ds(L, 1)]
                        e.dma_start(o_layer("win_sample")[:, :, 0:WINDOW - 1].rearrange("o b w k g d -> (o b) w (k g d)"),
                                    at_layer("cache_win")[:, :, 1:WINDOW].rearrange("o b w k g d -> (o b) w (k g d)")).then_inc(outs, 16)
                        e.dma_start(o_layer("conv_a_sample")[:, :, 0:CA - 2].rearrange("o b t d -> (o b) t d"),
                                    at_layer("state_conv_a")[:, :, 1:CA - 1].rearrange("o b t d -> (o b) t d")).then_inc(outs, 16)
                        e.dma_start(o_layer("conv_c_sample")[:, :, 0:CC - 2].rearrange("o b t d -> (o b) t d"),
                                    at_layer("state_conv_c")[:, :, 1:CC - 1].rearrange("o b t d -> (o b) t d")).then_inc(outs, 16)
                        e.wait_ge(nt_used, 11)
                        e.dma_start(o_layer("kv_prompt").rearrange("o i (t p) k g d -> p (o i t) (k g d)", p=P), nat[:, 0:4, 0:512]).then_inc(outs, 16)
                        e.dma_start(o_layer("win_prompt").rearrange("o i (t p) k g d -> p (o i t) (k g d)", p=P), nat[:, 0:4, 512:768]).then_inc(outs, 16)
                        e.dma_start(o_layer("kv_sample").rearrange("o b i k g d -> (o b i) (k g d)"), nat[0:NB, 4, 0:512]).then_inc(outs, 16)
                        e.dma_start(o_layer("win_sample")[:, :, WINDOW - 1:WINDOW].rearrange("o b w k g d -> (o b w) (k g d)"), nat[0:NB, 4, 512:768]).then_inc(outs, 16)
                        e.wait_ge(end_ready, 2)
                        e.dma_start(o_layer("conv_a_prompt").rearrange("o i t d -> (o i t) d"), ends[0:2, 0, :]).then_inc(outs, 16)
                        e.dma_start(o_layer("conv_a_sample")[:, :, CA - 2:CA - 1].rearrange("o b t d -> (o b t) d"), ends[2:10, 0, :]).then_inc(outs, 16)
                        e.dma_start(o_layer("conv_c_prompt").rearrange("o i t d -> (o i t) d"), ends[0:30, 1, :]).then_inc(outs, 16)
                        e.dma_start(o_layer("conv_c_sample")[:, :, CC - 2:CC - 1].rearrange("o b t d -> (o b t) d"), ends[30:38, 1, :]).then_inc(outs, 16)

                    @block.tensor
                    def _(e):
                        n = 0
                        for t in range(5):
                            w = P if t < 4 else NB
                            for q in range(2):
                                if n >= 2:
                                    e.wait_ge(nt_used, n - 1)
                                for i in range(4 if q == 0 else 2):
                                    mm = e.transpose(pa[n % 2][0:w, i * P:(i + 1) * P], z[:, Z_K + 4 * q + i, t * P:t * P + w], ident[:])
                                if q == 1 and t < 4:
                                    mm = e.transpose(pa[n % 2][0:w, 256:256 + NG_W], gateT[:, t * P:t * P + w], ident[0:NG_W, 0:NG_W])
                                mm.then_inc(nt_done, 1)
                                n += 1
                        e.wait_ge(st_l, 32)
                        for c in range(2):
                            e.transpose(pn[:, 0, c * 16:(c + 1) * 16], st_a[:, c * P:(c + 1) * P], ident[0:16, 0:16])
                        for q in range(2):
                            for c in range(2):
                                mm = e.transpose(pn[:, 1, (2 * q + c) * 120:(2 * q + c + 1) * 120], st_c[:, q, c * P:(c + 1) * P], ident[0:120, 0:120])
                        mm.then_inc(st_tr, 1)
                        e.wait_ge(w1l, 64)
                        pe = vecs[:, V_PE:V_END].rearrange("p (k h i) -> p k h i", k=2, h=2)
                        for kv in range(2):
                            for i in range(8):
                                mm = e.matmul(pg[:, 1, 0, 2 * kv:2 * kv + 2], w1[:, kv, i, :], pe[:, kv, :, i], start=i == 0, stop=i == 7)
                        mm.then_inc(pem, 1)
                        e.wait_ge(ua_ready, 1)
                        e.wait_ge(uc_ready, 2)
                        for c in range(2):
                            e.transpose(pg[0:10, 0, 0, c * P:(c + 1) * P], u_a[:, c, CA - 1 + 510:CA - 1 + TOK], ident[:])
                            mm = e.transpose(pg[0:38, 0, 1, c * P:(c + 1) * P], u_c[:, c, CC - 1 + 482:CC - 1 + TOK], ident[:])
                        mm.then_inc(end_tr, 1)

                    @block.scalar
                    def _(e):
                        e.activation(th[:], z[:, Z_C + 2:Z_C + 4, :], ACT.Tanh, scale=0.5).then_inc(tanh_c, 1)
                        n = 0
                        for t in range(5):
                            w = P if t < 4 else NB
                            for q in range(2):
                                e.wait_ge(nt_done, n + 1)
                                mm = e.copy(nat[0:w, t, 512 * q:512 + 256 * q], pa[n % 2][0:w, 0:512 - 256 * q])
                                if q == 1 and t < 4:
                                    mm = e.copy(gate_n[:, t, :], pa[n % 2][:, 256:256 + NG_W])
                                mm.then_inc(nt_used, 1)
                                n += 1
                        e.wait_ge(nt_used, 10)
                        e.copy(nat_new[:], nat[0:NB, 4, :]).then_inc(nt_used, 1)
                        e.wait_ge(pem, 1)
                        for i in range(4):
                            src = pg[64:128, 1, 0, i:i + 1] if i % 2 else pg[0:64, 1, 0, i:i + 1]
                            mm = e.copy(cb[:, i:i + 1], src)
                        mm.then_inc(cbs, 1)

                    @block.vector
                    def _(e):
                        link = lambda i: dve_chain(e, i)
                        link(e.memset(u_a[:, :, 0:CA - 1], 0.0))
                        link(e.memset(u_c[:, :, 0:CC - 1], 0.0))
                        e.tensor_tensor(u_a[:, :, CA - 1:], z[:, Z_A + 4:Z_A + 6, :], z[:, Z_A:Z_A + 2, :], ALU.mult).then_inc(ua_ready, 1)
                        e.wait_ge(tanh_c, 1)
                        e.scalar_tensor_tensor(u_c[:, :, CC - 1:], th[:], 1.0, z[:, Z_C:Z_C + 2, :], ALU.add, ALU.mult).then_inc(uc_ready, 1)
                        e.wait_ge(uc_ready, 1)
                        e.tensor_scalar(u_c[:, :, CC - 1:], u_c[:, :, CC - 1:], 0.5, None, ALU.mult).then_inc(uc_ready, 1)
                        e.wait_ge(uc_ready, 2)
                        e.wait_ge(ua_ready, 1)
                        e.wait_ge(st_tr, 1)
                        for c in range(2):
                            link(e.tensor_copy(us_a[:, c, 0:2, :].rearrange("p t b -> p b t"), pn[:, 0, c * 16:(c + 1) * 16].rearrange("p (b t) -> p b t", t=2)))
                            link(e.tensor_copy(us_a[:, c, 2, :], u_a[:, c, CA - 1 + SEQ:]))
                            for q in range(2):
                                link(e.tensor_copy(us_c[:, c, 0:30, 4 * q:4 * q + 4].rearrange("p t b -> p b t"),
                                                   pn[:, 1, (2 * q + c) * 120:(2 * q + c + 1) * 120].rearrange("p (b t) -> p b t", t=30)))
                            link(e.tensor_copy(us_c[:, c, 30, :], u_c[:, c, CC - 1 + SEQ:]))
                        for tap in range(CA):
                            for c in range(2):
                                w = vecs[:, V_CA + 2 * tap + c:V_CA + 2 * tap + c + 1]
                                for dst, src in ((y_a[:, c, 0:SEQ], u_a[:, c, tap:tap + SEQ]), (y_a[:, c, SEQ:], us_a[:, c, tap, :])):
                                    if tap == 0:
                                        link(e.tensor_scalar(dst, src, w, None, ALU.mult))
                                    else:
                                        link(e.scalar_tensor_tensor(dst, src, w, dst, ALU.mult, ALU.add))
                        link(e.tensor_tensor(oac[:, 4:6, :], y_a[:], z[:, Z_A + 2:Z_A + 4, :], ALU.mult))
                        link(e.tensor_copy(k_new[:, 0, :], z[:, Z_K + 2, SEQ:]))
                        link(e.tensor_copy(k_new[:, 1, :], z[:, Z_K + 4, SEQ:]))
                        link(e.memset(q_blk[:], 0.0))
                        for g in range(2):
                            r = slice(g * HD, (g + 1) * HD)
                            link(e.tensor_scalar(q_blk[r, :, g * HPG:(g + 1) * HPG].rearrange("p b i -> p i b"),
                                                 z[r, 0:HPG, SEQ:], HD ** -0.5, None, ALU.mult))
                        link(e.tensor_scalar(z[:, 0:4, 0:SEQ], z[:, 0:4, 0:SEQ], HD ** -0.5, None, ALU.mult))
                        e.wait_ge(w2l, 96)
                        link(e.tensor_scalar(w2[:], w2[:], 0.5, None, ALU.mult))
                        e.wait_ge(cbs, 1)
                        c4 = cb[:].rearrange("p (k h) -> p k h", h=2)
                        for g in range(2):
                            r = slice(g * 64, (g + 1) * 64)
                            link(e.tensor_tensor(cbias[r, :], c4[:, :, 0], c4[:, :, 1], ALU.add))
                        link(e.tensor_tensor(cbias[:], cbias[:], vecs[:, V_B1:V_B1 + 2], ALU.add))
                        e.wait_ge(end_tr, 1)
                        e.tensor_copy(ends[0:10, 0, :], pg[0:10, 0, 0, 0:256]).then_inc(end_ready, 1)
                        e.tensor_copy(ends[:, 1, :], pg[0:38, 0, 1, 0:256]).then_inc(end_ready, 1)

            NCH = SEQ // STRIDE
            with phase_semaphores(), ExitStack() as outer:
              with ExitStack() as scope:
                ck = sb(outer, "ck", [P, NCH])
                cv = sb(outer, "cv", [NCH, P])
                pairs = sb(scope, "pairs", [P, 8, 4, NCH])
                first = sb(scope, "first", [P, 2, NCH + 1])
                second = sb(scope, "second", [P, 2, NCH + 1])
                thp = sb(scope, "thp", [P, 2, NCH])
                pr_used, comp, half2, pre, thd, hid = (sem(n) for n in (
                    "pr_used", "comp", "half2", "pre", "thd", "hid"))
                cmp2, ck_ready, cv_ready = (sem(n) for n in ("cmp2", "ck_ready", "cv_ready"))

                def side_by_side(e, kv):
                    for q in range(2):
                        for g in range(2):
                            src = z[g * HD:(g + 1) * HD, Z_K + kv, 0:SEQ].rearrange("p (n i q) -> p q i n", i=8, q=2)[:, q]
                            dst = pairs[q * HD:(q + 1) * HD, :, 2 * kv + g, :]
                            (e.copy(dst, src) if e is nc.scalar else e.tensor_copy(dst, src)).then_inc(pr_used, 1)

                with nc.Block() as block:
                    @block.tensor
                    def _(e):
                        e.wait_ge(pr_used, 8)
                        for kv in range(2):
                            for i in range(8):
                                mm = e.matmul(pn[:, 0, kv * 64:(kv + 1) * 64], w1[:, kv, i, :], pairs[:, i, 2 * kv:2 * kv + 2, :],
                                              start=i == 0, stop=i == 7)
                        mm.then_inc(comp, 1)
                        e.wait_ge(hid, 1)
                        e.matmul(pa[0][:, 0:NCH], w2[:, 0, :], pairs[:, 0, 0, :], start=True, stop=True)
                        e.matmul(pa[1][0:NCH, 0:P], pairs[:, 0, 1, :], w2[:, 1, :], start=True, stop=True).then_inc(cmp2, 1)

                    @block.scalar
                    def _(e):
                        side_by_side(e, 1)
                        e.wait_ge(comp, 1)
                        src = pn[:, 0, 0:128].rearrange("p (k g n) -> p k g n", k=2, g=2)
                        for g in range(2):
                            e.copy(second[g * 64:(g + 1) * 64, :, 0:NCH], src[64:128, :, g, :]).then_inc(half2, 1)
                        e.wait_ge(pre, 1)
                        e.activation(thp[:], first[:, :, 0:NCH], ACT.Tanh, scale=0.5).then_inc(thd, 1)
                        e.wait_ge(cmp2, 1)
                        e.activation(ck[:], pa[0][:, 0:NCH], ACT.Identity, bias=vecs[:, V_B2:V_B2 + 1]).then_inc(ck_ready, 1)

                    @block.vector
                    def _(e):
                        link = lambda i: dve_chain(e, i)
                        link(e.memset(second[:], 0.0))
                        side_by_side(e, 0)
                        e.wait_ge(comp, 1)
                        src = pn[:, 0, 0:128].rearrange("p (k g n) -> p k g n", k=2, g=2)
                        for g in range(2):
                            link(e.tensor_copy(first[g * 64:(g + 1) * 64, :, 0:NCH], src[0:64, :, g, :]))
                        e.wait_ge(half2, 2)
                        link(e.tensor_tensor(first[:, :, 0:NCH], first[:, :, 0:NCH], second[:, :, 1:NCH + 1], ALU.add))
                        e.tensor_tensor(first[:, :, 0:NCH], first[:, :, 0:NCH],
                                        cbias[:].rearrange("p (k o) -> p k o", o=1).broadcast_to([P, 2, NCH]), ALU.add).then_inc(pre, 1)
                        e.wait_ge(thd, 1)
                        e.scalar_tensor_tensor(pairs[:, 0, 0:2, :], thp[:], 1.0, first[:, :, 0:NCH], ALU.add, ALU.mult).then_inc(hid, 1)
                        e.wait_ge(cmp2, 1)
                        e.tensor_tensor(cv[:], pa[1][0:NCH, 0:P], b2row[0:NCH, :], ALU.add).then_inc(cv_ready, 1)

              with ExitStack() as scope:
                toep_h = sb(scope, "toep_h", [P, 2, SEQ])
                s_lg = sb(scope, "s_lg", [P, 2, 2, SEQ])
                s_cm = sb(scope, "s_cm", [P, 2, NCH])
                mx = sb(scope, "mx", [P, 2, 3])
                nmx = sb(scope, "nmx", [P, 2, 3])
                den = sb(scope, "den", [P, 2, 3])
                coef = sb(scope, "coef", [P, 2, 3])
                pT = sb(scope, "pT", [P, 2, 2, SEQ])
                pTc = sb(scope, "pTc", [NCH, 2, P])
                q_i = sb(scope, "q_i", [P, SEQ])
                q_set = sem("q_set")
                toep_l = [sem("toep_l0"), sem("toep_l1")]
                logit, lg_read, expd, ptr, ptr_used, pv, o_read = (sem(n) for n in (
                    "logit", "lg_read", "expd", "ptr", "ptr_used", "pv", "o_read"))
                probs, ptc, ptc_used = sem("probs"), sem("ptc"), sem("ptc_used")
                STEPS = 2 * QT

                def blocks(t):
                    return 7 + 8 * t

                with nc.Block() as block:
                    @block.sync
                    def _(e):
                        def heads(i):
                            for g in range(2):
                                await_(e, lg_read, STEPS * i - STEPS + QT * (g + 1))
                                e.dma_start(toep_h[:, g, :], toep_dram.ap()[bass.ds(i + g * HPG, 1)].rearrange("o p q -> (o p) q")).then_inc(toep_l[g], 16)
                        for g in range(2):
                            e.dma_start(toep_h[:, g, :], toep_dram.ap()[g * HPG]).then_inc(toep_l[g], 16)
                        fori(e, 1, HPG, heads)
                        e.wait_ge(outs, 16 * 11)

                    def run(e, trip):
                        trip(0)
                        with e.Fori(1, HPG - 1) as i:
                            trip(i)
                        trip(HPG - 1, last=True)

                    def after(i, k, d):
                        return i + (k + d) // STEPS, (k + d) % STEPS

                    @block.tensor
                    def _(e):
                        def score(i, k):
                            g, t = k // QT, k % QT
                            r = slice(g * HD, (g + 1) * HD)
                            w = (t + 1) * P
                            n = STEPS * i + k
                            if not (isinstance(n, int) and n < 2):
                                await_(e, lg_read, n - 1)
                            if k == 0:
                                await_(e, q_set, i + 1)
                            q = q_i[r, t * P:(t + 1) * P]
                            e.matmul(pg[:, k % 2, 0, 0:w], q, z[r, Z_K + 2, 0:w], start=True, stop=True)
                            e.matmul(pg[:, k % 2, 1, 0:w], q, z[r, Z_K + 4, 0:w], start=True, stop=True)
                            if not (isinstance(n, int) and n < 3):
                                await_(e, ptc_used, n - 2)
                            await_(e, lg_read, n)
                            e.matmul(pa[1][:, (k % 2) * NCH:(k % 2) * NCH + blocks(t)], q, ck[r, 0:blocks(t)], start=True, stop=True).then_inc(logit, 1)

                        def turn(i, k):
                            t = k % QT
                            n = STEPS * i + k
                            await_(e, probs, n + 1)
                            await_(e, ptr_used, 2 * n)
                            for b in range(2):
                                for kt in range(t + 1):
                                    mm = e.transpose(pn[:, b, kt * P:(kt + 1) * P], s_lg[:, k % 2, b, kt * P:(kt + 1) * P], ident[:])
                            mm.then_inc(ptr, 1)

                        def values(i, k):
                            g, t = k // QT, k % QT
                            n = STEPS * i + k
                            if not (isinstance(n, int) and n == STEPS * HPG - 1):
                                await_(e, lg_read, n + 2)
                            e.transpose(pa[1][0:blocks(t), P:2 * P], s_cm[:, k % 2, 0:blocks(t)], ident[:]).then_inc(ptc, 1)
                            await_(e, ptr_used, 2 * n + 2)
                            await_(e, o_read, n)
                            r = slice(g * HD, (g + 1) * HD)
                            out = pa[0][r, 0:P]
                            for b in range(2):
                                for kt in range(t + 1):
                                    col = 128 * (3 if b == 0 else 5) + g * HD
                                    e.matmul(out, nat[:, kt, col:col + HD], pT[:, k % 2, b, kt * P:(kt + 1) * P],
                                             start=b == 0 and kt == 0, stop=False)
                            await_(e, ptc_used, n + 1)
                            e.matmul(out, cv[0:blocks(t), r], pTc[0:blocks(t), k % 2, :], start=False, stop=True).then_inc(pv, 1)

                        def trip(i, last=False):
                            for k in range(STEPS):
                                turn(i, k)
                                if not (last and k >= STEPS - 2):
                                    score(*after(i, k, 2))
                                values(i, k)
                        e.wait_ge(ck_ready, 1)
                        e.wait_ge(cv_ready, 1)
                        score(0, 0)
                        score(0, 1)
                        run(e, trip)

                    @block.vector
                    def _(e):
                        link = lambda x: dve_chain(e, x)

                        def read(i, k):
                            g, t = k // QT, k % QT
                            n = STEPS * i + k
                            w = (t + 1) * P
                            await_(e, logit, n + 1)
                            if t == 0:
                                await_(e, toep_l[g], 16 * (i + 1))
                            if not (isinstance(n, int) and n < 2):
                                await_(e, ptr, n - 1)
                                await_(e, ptc_used, n - 1)
                            bias = toep_h[:, g, SEQ - w:SEQ]
                            for b in range(2):
                                e.tensor_tensor_reduce(s_lg[:, k % 2, b, 0:w], pg[:, k % 2, b, 0:w], bias, 1.0, NEG,
                                                       ALU.add, ALU.max, mx[:, k % 2, b:b + 1])
                            link(e.tensor_tensor_reduce(s_cm[:, k % 2, 0:blocks(t)], pa[1][:, (k % 2) * NCH:(k % 2) * NCH + blocks(t)],
                                                        toep_h[:, g, 415 - P * t:SEQ:STRIDE], 1.0, NEG,
                                                        ALU.add, ALU.max, mx[:, k % 2, 2:3]))
                            e.tensor_scalar(nmx[:, k % 2, :], mx[:, k % 2, :], -1.0, -0.1 * NEG, ALU.mult, ALU.min).then_inc(lg_read, 1)

                        def normalise(i, k):
                            g, t = k // QT, k % QT
                            n = STEPS * i + k
                            w = (t + 1) * P
                            await_(e, expd, n + 1)
                            link(e.tensor_scalar(den[:, k % 2, :], den[:, k % 2, :], 1e-30, None, ALU.max))
                            link(e.reciprocal(den[:, k % 2, :], den[:, k % 2, :]))
                            gates = gate_n[:, t, :].rearrange("p (b h) -> p b h", b=3)
                            head = slice(i + g * HPG, i + g * HPG + 1) if isinstance(i, int) else bass.ds(i + g * HPG, 1)
                            gv = gates[:, :, head].rearrange("p b o -> p (b o)")
                            cf = coef[:, k % 2, :]
                            link(e.tensor_tensor(cf, den[:, k % 2, :], gv, ALU.mult))
                            e.tensor_scalar(s_lg[:, k % 2, 0, 0:w], s_lg[:, k % 2, 0, 0:w], cf[:, 1:2], None, ALU.mult)
                            e.tensor_scalar(s_cm[:, k % 2, 0:blocks(t)], s_cm[:, k % 2, 0:blocks(t)], cf[:, 0:1], None, ALU.mult)
                            e.tensor_scalar(s_lg[:, k % 2, 1, 0:w], s_lg[:, k % 2, 1, 0:w], cf[:, 2:3], None, ALU.mult).then_inc(probs, 1)

                        def copy(i, k):
                            w = (k % QT + 1) * P
                            await_(e, ptr, STEPS * i + k + 1)
                            e.tensor_copy(pT[:, k % 2, 1, 0:w], pn[:, 1, 0:w]).then_inc(ptr_used, 1)

                        def keep(i, k):
                            g, t = k // QT, k % QT
                            await_(e, pv, STEPS * i + k + 1)
                            r = slice(g * HD, (g + 1) * HD)
                            at = slice(i, i + 1) if isinstance(i, int) else bass.ds(i, 1)
                            e.tensor_copy(oac[r, at, t * P:(t + 1) * P].rearrange("p o q -> p (o q)"), pa[0][r, 0:P]).then_inc(o_read, 1)

                        def trip(i, last=False):
                            for k in range(STEPS):
                                dve_chain.restart(e)
                                normalise(i, k)
                                if not (last and k == STEPS - 1):
                                    read(*after(i, k, 1))
                                copy(i, k)
                                if not (isinstance(i, int) and i == k == 0):
                                    keep(*after(i, k, -1))
                        dve_chain.restart(e)
                        read(0, 0)
                        run(e, trip)
                        keep(HPG - 1, STEPS - 1)

                    @block.scalar
                    def _(e):
                        def queries(i):
                            await_(e, logit, STEPS * i)
                            at = slice(i, i + 1) if isinstance(i, int) else bass.ds(i, 1)
                            e.copy(q_i[:], z[:, at, 0:SEQ].rearrange("p o q -> p (o q)")).then_inc(q_set, 1)

                        def exps(i, k):
                            t = k % QT
                            n = STEPS * i + k
                            w = (t + 1) * P
                            await_(e, lg_read, n + 1)
                            for b in range(2):
                                e.activation(s_lg[:, k % 2, b, 0:w], s_lg[:, k % 2, b, 0:w], ACT.Exp,
                                             bias=nmx[:, k % 2, b:b + 1], accum_out=den[:, k % 2, 1 + b:2 + b])
                            e.activation(s_cm[:, k % 2, 0:blocks(t)], s_cm[:, k % 2, 0:blocks(t)], ACT.Exp,
                                         bias=nmx[:, k % 2, 2:3], accum_out=den[:, k % 2, 0:1]).then_inc(expd, 1)

                        def copy(i, k):
                            t = k % QT
                            n = STEPS * i + k
                            w = (t + 1) * P
                            await_(e, ptr, n + 1)
                            if not (isinstance(n, int) and n < 2):
                                await_(e, pv, n - 1)
                            e.copy(pT[:, k % 2, 0, 0:w], pn[:, 0, 0:w]).then_inc(ptr_used, 1)

                        def copy_compressed(i, k):
                            await_(e, ptc, STEPS * i + k + 1)
                            e.copy(pTc[0:blocks(k % QT), k % 2, :], pa[1][0:blocks(k % QT), P:2 * P]).then_inc(ptc_used, 1)

                        def trip(i, last=False):
                            for k in range(STEPS):
                                copy(i, k)
                                if k == STEPS - 2 and not last:
                                    queries(i + 1)
                                if not (last and k == STEPS - 1):
                                    exps(*after(i, k, 1))
                                copy_compressed(i, k)
                        queries(0)
                        exps(0, 0)
                        run(e, trip)
            upto_b2.close()

            with phase_semaphores(), ExitStack() as scope:
                TILES = 8
                cache = sb(scope, "cache", [P, 4, 4 * 512])
                cell = sb(scope, "cell", [P, 4], U32)
                v_sel = sb(scope, "v_sel", [P, 2, 32, P])
                apart = sb(scope, "apart", [P, 2, 4, 4, HD])
                win = sb(scope, "win", [P, 2, 4, 2 * P])
                xkv = (w_raw[:, 1, :].rearrange("p (k n) -> p k n", k=2), sb(scope, "xkv", [P, 2, 512]))
                k_sel = w_raw[:, 2, 0:512]
                first = w_raw[:, 2, 512:1024].rearrange("p (k n) -> p k n", k=2)
                second = w_raw[:, 3, 0:2 * (2 * P + 1)].rearrange("p (k n) -> p k n", k=2)
                ck = w_raw[:, 3, 2 * (2 * P + 1):2 * (2 * P + 1) + 2 * P]
                cv = sb(scope, "cvs", [P, 2, P])
                lc = sb(scope, "lc", [P, 2, N_HEADS])
                lg = sb(scope, "lg", [P, BLK, N_HEADS])
                pr = sb(scope, "pr", [P, BLK, N_HEADS])
                mxs = sb(scope, "mxs", [P, 3, N_HEADS])
                top = sb(scope, "top", [16, 2])
                dg = sb(scope, "dg", [16, 2, 16])
                sums = sb(scope, "sums", [P, 3, N_HEADS])
                inv = sb(scope, "inv", [P, 3, N_HEADS])
                pgrp = sb(scope, "pgrp", [P, 2, N_KV])
                score = sb(scope, "score", [N_KV, SELB + 1])
                top8 = sb(scope, "top8", [N_KV, 2, 8])
                penT = sb(scope, "penT", [SELB + 1, N_KV])
                pen = sb(scope, "pen", [P, 2, N_KV])
                gate_dg = w_raw[0:NG_W, 1, 0:NB * NG_W].rearrange("p (b c) -> p b c", b=NB)
                gate_bc = w_raw[:, 3, 4 * P + 2 + 2 * P:4 * P + 2 + 2 * P + NB * NG_W].rearrange("p (b c) -> p b c", b=NB)
                coefs = sb(scope, "coefs", [P, 3, N_HEADS])
                o24 = sb(scope, "o24", [P, 3, N_HEADS])
                o8 = sb(scope, "o8", [P, N_HEADS])
                got = [sem(f"got{i}") for i in range(4)]
                (cell_set, v_kept, staged, tr_k, tr_v, tr_s, xk_ready, xv_ready, ks_ready, xkv_used, ks_used, c_read, pre_s, th_s, hid_s,
                 cmp_s, ck_s, cv_s, sc_done, mxc, mxt, dgc, mbc, lc_in, lc_exp, sumc, denc, pcn, blk_score, penal, pen_tr, penT_s, pen_bc,
                 s_taken, s_done, mxw, mxwt, dgw, mbw, lg_in, lg_exp, sumw, denw, pv_done, o_done, gate_s, gate_mm) = (
                    sem(n) for n in ("cell_set", "v_kept", "staged", "tr_k", "tr_v", "tr_s", "xk_ready", "xv_ready", "ks_ready", "xkv_used", "ks_used",
                                     "c_read", "pre_s", "th_s", "hid_s", "cmp_s", "ck_s", "cv_s", "sc_done", "mxc", "mxt", "dgc", "mbc",
                                     "lc_in", "lc_exp", "sumc", "denc", "pcn", "blk_score", "penal", "pen_tr", "penT_s", "pen_bc", "s_taken",
                                     "s_done", "mxw", "mxwt", "dgw", "mbw", "lg_in", "lg_exp", "sumw", "denw", "pv_done",
                                     "o_done", "gate_s", "gate_mm"))
                rows_dram = A["cache_kv"].rearrange("l n (r t) k g d -> (l n r) (t k g d)", t=4)

                win_in = [sem("win_in0"), sem("win_in1")]

                def in_turn(e, tiles, chain):
                    def trip(b, par):
                        restart_chain(e)
                        tiles(b, par, lambda slot: chain(b - 1, 1 - par, slot))
                    tiles(0, 0, lambda slot: None)
                    trip(1, 1)
                    trip(2, 0)
                    with e.Fori(1, NB // 2 - 1) as j:
                        trip(2 * j + 1, 1)
                        trip(2 * j + 2, 0)
                    trip(NB - 1, 1)
                    restart_chain(e)
                    for slot in range(2 * TILES + 2):
                        chain(NB - 1, 1, slot)

                def restart_chain(e):
                    if e is nc.vector:
                        dve_chain.restart(e)

                with nc.Block() as block:
                    @block.sync
                    def _(e):
                        def window(b, par):
                            src = A["cache_win"][bass.ds(L, 1), bass.ds(b, 1)].rearrange("l o (p t) k g d -> (l o p) t (k g d)", t=4)
                            e.dma_start(win[:, par], src).then_inc(win_in[par], 16)
                        window(0, 0)
                        window(1, 1)
                        with e.Fori(1, NB // 2) as j:
                            for par in range(2):
                                await_(e, pv_done, 2 * j + par - 1)
                                window(2 * j + par, par)

                    @block.gpsimd
                    def _(e):
                        def gather(b, k):
                            e.tensor_copy(cell[:, k % 4:k % 4 + 1], gather_rows[:, bass.ds(b * TILES + k, 1)]).then_inc(cell_set, 1)
                            await_(e, cell_set, b * TILES + k + 1)
                            e.indirect_dma_start(out=cache[:, k % 4, :], out_offset=None, in_=rows_dram,
                                                 in_offset=bass.IndirectOffsetOnAxis(ap=cell[:, k % 4:k % 4 + 1], axis=0)).then_inc(got[k % 4], 16)

                        def trip(b, par, last=False):
                            for k in range(TILES):
                                await_(e, got[k % 4], b * 32 + 16 * (k // 4 + 1))
                                if k == 0 and not (isinstance(b, int) and b < 2):
                                    await_(e, pv_done, b - 1)
                                src = cache[:, k % 4, :].rearrange("p (t x) -> p t x", t=4)[:, :, 384:512]
                                e.tensor_copy(v_sel[:, par, 4 * k:4 * k + 4, :], src).then_inc(v_kept, 1)
                                if k < 4 or not last:
                                    await_(e, tr_s, b * (TILES + 1) + k + 1)
                                    await_(e, v_kept, b * TILES + k + 1)
                                    gather(b, k + 4)
                        for k in range(4):
                            gather(0, k)
                        trip(0, 0)
                        trip(1, 1)
                        with e.Fori(1, NB // 2 - 1) as j:
                            trip(2 * j, 0)
                            trip(2 * j + 1, 1)
                        trip(NB - 2, 0)
                        trip(NB - 1, 1, last=True)

                    @block.tensor
                    def _(e):
                        e.wait_ge(gate_s, 1)
                        e.matmul(pa[0][:, 0:NB * NG_W], ones[0:NG_W, :], gate_dg[:].rearrange("p b c -> p (b c)"), start=True, stop=True).then_inc(gate_mm, 1)
                        e.wait_ge(gate_mm, 1)

                        def q_of(b):
                            if isinstance(b, int):
                                return q_blk[:, b, :]
                            return q_blk[:, bass.ds(b, 1), :].rearrange("p o h -> p (o h)")

                        def turn(b, k):
                            n = b * TILES + k
                            await_(e, staged, n + 1)
                            src = cache[:, k % 4, :].rearrange("p (t x) -> p t x", t=4)
                            for kv, done, used in ((0, tr_k, xk_ready), (1, tr_v, xv_ready)):
                                await_(e, used, n)
                                for pair in range(2):
                                    for g in range(2):
                                        at = (2 * pair + g) * P
                                        mm = e.transpose(pg[:, 0, kv, at:at + P],
                                                         apart[:, k % 2, 2 * kv + g, 2 * pair:2 * pair + 2, :].rearrange("p t d -> p (t d)"), ident[:])
                                mm.then_inc(done, 1)
                            await_(e, ks_ready, b * (TILES + 1) + k)
                            for t in range(4):
                                mm = e.transpose(pg[:, 1, 0, t * P:(t + 1) * P], src[:, t, 256:384], ident[:])
                            mm.then_inc(tr_s, 1)

                        def use(b, k):
                            n = b * TILES + k
                            if k % 4 == 0:
                                await_(e, c_read, 2 * (2 * b + k // 4))
                            for kv, ready in ((0, xk_ready), (1, xv_ready)):
                                await_(e, ready, n + 1)
                                for pair in range(2):
                                    e.matmul(pg[:, 1, 1, kv * 256:(kv + 1) * 256], w1[:, kv, 2 * (k % 4) + pair, :],
                                             xkv[k % 2][:, kv, pair * 256:(pair + 1) * 256],
                                             start=k % 4 == 0 and kv == 0 and pair == 0, stop=k % 4 == 3 and pair == 1, skip_group_check=True
                                             ).then_inc(xkv_used, 1)
                            await_(e, ks_ready, b * (TILES + 1) + k + 1)
                            if k == 0:
                                await_(e, s_taken, b)
                            for t in range(4):
                                mm = e.matmul(pn[:, 0, (4 * k + t) * 8:(4 * k + t + 1) * 8], k_sel[:, t * P:(t + 1) * P], q_of(b), start=True, stop=True)
                            mm.then_inc(ks_used, 1)

                        def tiles(b, par, chain):
                            for k in range(TILES):
                                turn(b, k)
                                chain(2 * k)
                                if k >= 1:
                                    use(b, k - 1)
                                chain(2 * k + 1)
                            await_(e, win_in[par], 8 * (b - par) + 16)
                            await_(e, ks_ready, b * (TILES + 1) + TILES)
                            for t in range(4):
                                mm = e.transpose(pg[:, 1, 0, t * P:(t + 1) * P], win[:, par, t, 0:P], ident[:])
                            mm.then_inc(tr_s, 1)
                            chain(2 * TILES)
                            use(b, TILES - 1)
                            chain(2 * TILES + 1)
                            await_(e, ks_ready, (b + 1) * (TILES + 1))
                            for t in range(4):
                                mm = e.matmul(pn[:, 0, (WIN0 + t) * 8:(WIN0 + t + 1) * 8], k_sel[:, t * P:(t + 1) * P], q_of(b), start=True, stop=True)
                            mm.then_inc(ks_used, 1)
                            e.matmul(pn[0:NB, 0, NEWS * 8:NEWS * 8 + 8], k_new[:, 0, :], q_of(b), start=True, stop=True)
                            e.matmul(pn[0:NB, 0, NEWW * 8:NEWW * 8 + 8], k_new[:, 1, :], q_of(b), start=True, stop=True).then_inc(s_done, 1)

                        def chain(b, par, slot):
                            if slot == 0:
                                await_(e, hid_s, b + 1)
                                await_(e, o_done, b)
                                e.matmul(pa[0][:, 0:256], w2[:, 0, :], first[:, 0, :], start=True, stop=True)
                                for t in range(2):
                                    mm = e.matmul(pn[:, 1, t * P:(t + 1) * P], first[:, 1, t * P:(t + 1) * P], w2[:, 1, :], start=True, stop=True)
                                mm.then_inc(cmp_s, 1)
                            elif slot == 1:
                                await_(e, ck_s, b + 1)
                                for t in range(2):
                                    mm = e.matmul(pa[1][:, t * 8:(t + 1) * 8], ck[:, t * P:(t + 1) * P], q_of(b), start=True, stop=True)
                                mm.then_inc(sc_done, 1)
                            elif slot == 2:
                                await_(e, mxc, b + 1)
                                e.transpose(pa[1][0:8, 128:256], mxs[:, 0, :], ident[:]).then_inc(mxt, 1)
                            elif slot == 3:
                                await_(e, dgc, b + 1)
                                e.matmul(pa[1][:, 32:40], ones[0:8, :], dg[0:8, 0, 0:8], start=True, stop=True).then_inc(mbc, 1)
                            elif slot == 4:
                                await_(e, sumc, b + 1)
                                e.matmul(pa[1][:, 40:48], ones[:], sums[:, 0, :], start=True, stop=True).then_inc(denc, 1)
                            elif slot == 5:
                                await_(e, pcn, b + 1)
                                for t in range(2):
                                    mm = e.matmul(pa[1][0:N_KV, 256:256 + SELB + 1], pgrp[:, t, :], ov[:, t, :], start=t == 0, stop=t == 1)
                                mm.then_inc(blk_score, 1)
                            elif slot == 6:
                                await_(e, penal, b + 1)
                                e.transpose(pa[1][0:SELB + 1, 64:66], score[:], ident[0:N_KV, 0:N_KV]).then_inc(pen_tr, 1)
                            elif slot == 7:
                                await_(e, penT_s, b + 1)
                                for t in range(2):
                                    mm = e.matmul(pa[1][:, 48 + 2 * t:50 + 2 * t], rt[:, t * P:(t + 1) * P], penT[:], start=True, stop=True)
                                mm.then_inc(pen_bc, 1)
                            elif slot == 8:
                                await_(e, mxw, b + 1)
                                e.transpose(pa[1][0:16, 128:256], mxs[:, 1:3, :].rearrange("p a h -> p (a h)"), ident[:]).then_inc(mxwt, 1)
                            elif slot == 9:
                                await_(e, dgw, b + 1)
                                e.matmul(pa[1][:, 0:16], ones[0:16, :], dg[:, 1, :], start=True, stop=True).then_inc(mbw, 1)
                            elif slot == 10:
                                await_(e, sumw, b + 1)
                                e.matmul(pa[1][:, 16:32], ones[:], sums[:, 1:3, :].rearrange("p a h -> p (a h)"), start=True, stop=True).then_inc(denw, 1)
                            elif slot == 11:
                                await_(e, v_kept, TILES * b + TILES)
                                for t in range(2):
                                    e.matmul(pn[:, 1, 0:8], cv[:, t, :], lc[:, t, :], start=t == 0, stop=t == 1)
                                for t in range(32):
                                    e.matmul(pn[:, 1, 8:16], v_sel[:, par, t, :], pr[:, t, :], start=t == 0, stop=False)
                                e.matmul(pn[:, 1, 8:16], nat_new[:, 384:512], pr[0:NB, NEWS, :], start=False, stop=True)
                                for t in range(4):
                                    e.matmul(pn[:, 1, 16:24], win[:, par, t, P:2 * P], pr[:, WIN0 + t, :], start=t == 0, stop=False)
                                e.matmul(pn[:, 1, 16:24], nat_new[:, 640:768], pr[0:NB, NEWW, :], start=False, stop=True).then_inc(pv_done, 1)
                        in_turn(e, tiles, chain)

                    @block.scalar
                    def _(e):
                        def tiles(b, par, chain):
                            def half(t):
                                await_(e, xkv_used, 4 * (b * TILES + 4 * t + 4))
                                src = pg[:, 1, 1, :].rearrange("p (k g c) -> p k g c", k=2, g=2)
                                for g in range(2):
                                    mm = e.copy(second[g * 64:(g + 1) * 64, :, t * P:(t + 1) * P], src[64:128, :, g, :])
                                mm.then_inc(c_read, 1)
                            for k in range(TILES + 1):
                                chain(2 * k)
                                if k < TILES:
                                    n = b * TILES + k
                                    await_(e, tr_k, n + 1)
                                    if not (isinstance(b, int) and n < 2):
                                        await_(e, xkv_used, 4 * n - 4)
                                    e.copy(xkv[k % 2][:, 0, :], pg[:, 0, 0, :]).then_inc(xk_ready, 1)
                                m = b * (TILES + 1) + k
                                await_(e, tr_s, m + 1)
                                await_(e, ks_used, m)
                                e.copy(k_sel[:], pg[:, 1, 0, :]).then_inc(ks_ready, 1)
                                chain(2 * k + 1)
                                if k == 4:
                                    half(0)
                            half(1)

                        def chain(b, par, slot):
                            if slot == 0:
                                await_(e, pre_s, b + 1)
                                e.activation(second[:, :, 0:2 * P], first[:], ACT.Tanh, scale=0.5).then_inc(th_s, 1)
                            elif slot == 1:
                                await_(e, cmp_s, b + 1)
                                e.activation(ck[:], pa[0][:, 0:256], ACT.Identity, bias=vecs[:, V_B2:V_B2 + 1]).then_inc(ck_s, 1)
                            elif slot == 4:
                                await_(e, lc_in, b + 1)
                                e.activation(lc[:], lc[:], ACT.Exp).then_inc(lc_exp, 1)
                            elif slot == 10:
                                await_(e, lg_in, b + 1)
                                e.activation(pr[:], lg[:], ACT.Exp).then_inc(lg_exp, 1)
                        in_turn(e, tiles, chain)

                    @block.vector
                    def _(e):
                        link = lambda x: dve_chain(e, x)
                        link(e.memset(second[:], 0.0))
                        link(e.memset(lg[:], NEG))
                        e.tensor_tensor(gate_dg[:], gateT[:, SEQ:].rearrange("p (b o) -> p b o", o=1).broadcast_to([NG_W, NB, NG_W]),
                                        ident[0:NG_W, 0:NG_W].rearrange("p (o c) -> p o c", o=1).broadcast_to([NG_W, NB, NG_W]), ALU.mult).then_inc(gate_s, 1)
                        e.wait_ge(gate_mm, 1)
                        link(e.tensor_copy(gate_bc[:].rearrange("p b c -> p (b c)"), pa[0][:, 0:NB * NG_W]))

                        def bc(ap, n):
                            return ap.rearrange("p (o h) -> p o h", o=1).broadcast_to([P, n, N_HEADS])

                        def tiles(b, par, chain):
                            def half(t):
                                await_(e, xkv_used, 4 * (b * TILES + 4 * t + 4))
                                src = pg[:, 1, 1, :].rearrange("p (k g c) -> p k g c", k=2, g=2)
                                for g in range(2):
                                    mm = e.tensor_copy(first[g * 64:(g + 1) * 64, :, t * P:(t + 1) * P], src[0:64, :, g, :])
                                mm.then_inc(c_read, 1)

                            def stage(k):
                                n = b * TILES + k
                                await_(e, got[k % 4], b * 32 + 16 * (k // 4 + 1))
                                if not (isinstance(b, int) and n < 2):
                                    await_(e, tr_v, n - 1)
                                e.tensor_copy(apart[:, k % 2].rearrange("p x t d -> p t x d"),
                                              cache[:, k % 4, :].rearrange("p (t x) -> p t x", t=4)[:, :, 0:256].rearrange("p t (x d) -> p t x d", d=HD)
                                              ).then_inc(staged, 1)
                            stage(0)
                            for k in range(TILES + 1):
                                chain(2 * k)
                                if k < TILES:
                                    n = b * TILES + k
                                    if k + 1 < TILES:
                                        stage(k + 1)
                                    await_(e, tr_v, n + 1)
                                    if not (isinstance(b, int) and n < 2):
                                        await_(e, xkv_used, 4 * n - 4)
                                    e.tensor_copy(xkv[k % 2][:, 1, :], pg[:, 0, 1, :]).then_inc(xv_ready, 1)
                                chain(2 * k + 1)
                                if k == 4:
                                    half(0)
                            half(1)

                        def chain(b, par, slot):
                            if slot == 0:
                                await_(e, c_read, 4 * b + 4)
                                link(e.tensor_tensor(first[:], first[:], second[:, :, 1:2 * P + 1], ALU.add))
                                e.tensor_tensor(first[:], first[:], cbias[:].rearrange("p (k o) -> p k o", o=1).broadcast_to([P, 2, 2 * P]), ALU.add).then_inc(pre_s, 1)
                                await_(e, th_s, b + 1)
                                e.scalar_tensor_tensor(first[:], second[:, :, 0:2 * P], 1.0, first[:], ALU.add, ALU.mult).then_inc(hid_s, 1)
                                await_(e, s_done, b + 1)
                                s3 = pn[:, 0, 0:BLK * 8].rearrange("p (b h) -> p b h", h=N_HEADS)
                                e.tensor_tensor(lg[:, 0:32, :], s3[:, 0:32, :], key_bias[:, 0:32, :], ALU.add)
                                e.tensor_tensor(lg[:, WIN0:WIN0 + 4, :], s3[:, WIN0:WIN0 + 4, :], key_bias[:, WIN0:WIN0 + 4, :], ALU.add)
                                nb = new_bias[:, b:b + 1, :] if isinstance(b, int) else new_bias[:, bass.ds(b, 1), :]
                                e.tensor_tensor(lg[0:NB, NEWS:NEWS + 1, :], s3[0:NB, NEWS:NEWS + 1, :], nb, ALU.add)
                                e.tensor_tensor(lg[0:NB, NEWW:NEWW + 1, :], s3[0:NB, NEWW:NEWW + 1, :], nb, ALU.add).then_inc(s_taken, 1)
                            elif slot == 1:
                                await_(e, cmp_s, b + 1)
                                e.tensor_tensor(cv[:], pn[:, 1, 0:256].rearrange("p (t x) -> p t x", t=2),
                                                b2row[:].rearrange("p (o x) -> p o x", o=1).broadcast_to([P, 2, P]), ALU.add).then_inc(cv_s, 1)
                            elif slot == 2:
                                await_(e, sc_done, b + 1)
                                link(e.tensor_tensor(lc[:], pa[1][:, 0:16].rearrange("p (t h) -> p t h", t=2), key_bias[:, BLK:BLK + 2, :], ALU.add))
                                e.tensor_tensor(mxs[:, 0, :], lc[:, 0, :], lc[:, 1, :], ALU.max).then_inc(mxc, 1)
                            elif slot == 3:
                                await_(e, mxt, b + 1)
                                link(e.tensor_reduce(top[0:8, 0:1], pa[1][0:8, 128:256], AX.X, ALU.max))
                                e.tensor_scalar(dg[0:8, 0, 0:8], ident[0:8, 0:8], top[0:8, 0:1], None, ALU.mult).then_inc(dgc, 1)
                            elif slot == 4:
                                await_(e, mbc, b + 1)
                                e.tensor_tensor(lc[:], lc[:], bc(pa[1][:, 32:40], 2), ALU.subtract).then_inc(lc_in, 1)
                                await_(e, lc_exp, b + 1)
                                e.tensor_tensor(sums[:, 0, :], lc[:, 0, :], lc[:, 1, :], ALU.add).then_inc(sumc, 1)
                            elif slot == 5:
                                await_(e, denc, b + 1)
                                link(e.reciprocal(inv[:, 0, :], pa[1][:, 40:48]))
                                link(e.tensor_tensor(lc[:], lc[:], bc(inv[:, 0, :], 2), ALU.mult))
                                e.tensor_reduce(pgrp[:], lc[:].rearrange("p t (g i) -> p t g i", g=2), AX.X, ALU.add).then_inc(pcn, 1)
                            elif slot == 6:
                                await_(e, blk_score, b + 1)
                                link(e.tensor_copy(score[:], pa[1][0:N_KV, 256:256 + SELB + 1]))
                                link(e.memset(score[:, 0:1], SEL_FORCE))
                                link(e.memset(score[:, SELB - 1:SELB + 1], SEL_FORCE))
                                for r in range(N_SEL // 8):
                                    link(e.max(top8[:, r, :], score[:]))
                                    link(e.match_replace(score[:], top8[:, r, :], score[:], -1.0))
                                e.tensor_scalar(score[:], score[:], 0.0, NEG, ALU.is_ge, ALU.mult).then_inc(penal, 1)
                            elif slot == 7:
                                await_(e, pen_tr, b + 1)
                                e.tensor_copy(penT[:], pa[1][0:SELB + 1, 64:66]).then_inc(penT_s, 1)
                            elif slot == 8:
                                await_(e, pen_bc, b + 1)
                                link(e.tensor_copy(pen[:].rearrange("p t g -> p (t g)"), pa[1][:, 48:52]))
                                await_(e, s_taken, b + 1)
                                for t in range(2):
                                    for g in range(2):
                                        hs, bs = slice(g * HPG, (g + 1) * HPG), slice(16 * t, 16 * t + 16)
                                        mm = e.tensor_scalar(lg[:, bs, hs], lg[:, bs, hs], pen[:, t, g:g + 1], None, ALU.add)
                                link(mm)
                                e.tensor_reduce(mxs[:, 1, :], lg[:, 0:WIN0, :].rearrange("p b h -> p h b"), AX.X, ALU.max)
                                e.tensor_reduce(mxs[:, 2, :], lg[:, WIN0:BLK, :].rearrange("p b h -> p h b"), AX.X, ALU.max).then_inc(mxw, 1)
                            elif slot == 9:
                                await_(e, mxwt, b + 1)
                                link(e.tensor_reduce(top[:, 1:2], pa[1][0:16, 128:256], AX.X, ALU.max))
                                e.tensor_scalar(dg[:, 1, :], ident[0:16, 0:16], top[:, 1:2], None, ALU.mult).then_inc(dgw, 1)
                            elif slot == 10:
                                await_(e, mbw, b + 1)
                                e.tensor_tensor(lg[:, 0:WIN0, :], lg[:, 0:WIN0, :], bc(pa[1][:, 0:8], WIN0), ALU.subtract)
                                e.tensor_tensor(lg[:, WIN0:BLK, :], lg[:, WIN0:BLK, :], bc(pa[1][:, 8:16], BLK - WIN0), ALU.subtract).then_inc(lg_in, 1)
                                await_(e, lg_exp, b + 1)
                                e.tensor_reduce(sums[:, 1, :], pr[:, 0:WIN0, :].rearrange("p b h -> p h b"), AX.X, ALU.add)
                                e.tensor_reduce(sums[:, 2, :], pr[:, WIN0:BLK, :].rearrange("p b h -> p h b"), AX.X, ALU.add).then_inc(sumw, 1)
                            elif slot == 11:
                                await_(e, denw, b + 1)
                                link(e.reciprocal(inv[:, 1:3, :].rearrange("p a h -> p (a h)"), pa[1][:, 16:32]))
                                gb = gate_bc[:, b:b + 1, :] if isinstance(b, int) else gate_bc[:, bass.ds(b, 1), :]
                                link(e.tensor_copy(coefs[:], gb.rearrange("p o (a h) -> p (o a) h", a=3)))
                                link(e.tensor_tensor(coefs[:, 1:3, :], coefs[:, 1:3, :], inv[:, 1:3, :], ALU.mult))
                            elif slot == 12:
                                await_(e, pv_done, b + 1)
                                link(e.tensor_tensor(o24[:], coefs[:], pn[:, 1, 0:24].rearrange("p (a h) -> p a h", a=3), ALU.mult))
                                link(e.tensor_reduce(o8[:], o24[:].rearrange("p a h -> p h a"), AX.X, ALU.add))
                                for g in range(2):
                                    r = slice(g * HD, (g + 1) * HD)
                                    at = slice(b + SEQ, b + SEQ + 1) if isinstance(b, int) else bass.ds(b + SEQ, 1)
                                    mm = e.tensor_copy(oac[r, 0:HPG, at], o8[r, g * HPG:(g + 1) * HPG].rearrange("p (i o) -> p i o", o=1))
                                mm.then_inc(o_done, 1)
                        dve_chain.restart(e)
                        in_turn(e, tiles, chain)
                        dve_chain.restart(e)
                        link(e.tensor_scalar(gather_rows[:], gather_rows[:], float(POOL * 32), None, ALU.add))
            upto_b3.close()

            converted = [0]

            def stage_block(u0, n, load, act_step, dve_step=lambda e, j, s: None, source=None, chunks=KC, scale=1.0,
                            operand=(act_hi, act_lo), pe=None, last=None, unroll=False):
                base = converted[0]
                if source is not None:
                    converted[0] += chunks
                with nc.Block() as block:
                    @block.sync
                    def _(e):
                        load(e)

                    @block.scalar
                    def _(e):
                        if source is not None:
                            for c in range(chunks):
                                e.activation(operand[0][:, c, :], source(c), ACT.Copy, scale=scale).then_inc(op_hi, 1)
                        if last is None:
                            unit_groups(e, u0, n, lambda v, slot, full: split_hi(e, v, slot, full), lambda j, s: act_step(e, j, s))
                        else:
                            last(e, lambda v, slot, full: split_hi(e, v, slot, full), lambda m: act_step(e, m))

                    @block.vector
                    def _(e):
                        if source is not None:
                            for c in range(chunks):
                                e.wait_ge(op_hi, base + c + 1)
                                e.scalar_tensor_tensor(operand[1][:, c, :], source(c), scale, operand[0][:, c, :].bitcast(F32),
                                                       ALU.mult, ALU.subtract).then_inc(op_lo, 1)
                        if last is None:
                            unit_groups(e, u0, n, lambda v, slot, full: split_lo(e, v, slot), lambda j, s: dve_step(e, j, s), unroll=unroll)
                        else:
                            last(e, lambda v, slot, full: split_lo(e, v, slot), lambda m: None)

                    @block.tensor
                    def _(e):
                        if source is not None:
                            e.wait_ge(op_lo, base + chunks)
                        pe(e)

            def tile_to(dst, u0, width=None):
                def step(e, j, s):
                    tile_done_(e, u0 + RING * j + s)
                    to = dst[:, bass.ds(RING * j + s, 1), :].rearrange("p o t -> p (o t)")
                    if width is None:
                        e.copy(halves(to), out_tile(s % 2)).then_inc(evac[s % 2], 1)
                    else:
                        e.copy(to, pg[:, s % 2, 0, 0:width]).then_inc(evac[s % 2], 1)
                return step

            with ExitStack() as scope:
                G = sb(scope, "G", [P, 3 * KC, TOK])
                y_c = sb(scope, "y_c", [P, 2, TOK])
                sq_c = sb(scope, "sq_c", [P, 2, TOK])
                diag_c = sb(scope, "diag_c", [P, TOK])
                ms_c = sb(scope, "ms_c", [P, NB])
                r_c = sb(scope, "r_c", [P, NB])
                yc_ready, mean_c, xc_ready, sqc, var_c, msc, rc, dgcc, rbc, xn, vc, thv = (sem(n) for n in (
                    "yc_ready", "mean_c", "xc_ready", "sqc", "var_c", "msc", "rc", "dgcc", "rbc", "xn", "vc", "thv"))
                op_hi, op_lo, merged = sem("op_hi"), sem("op_lo"), sem("merged")

                def load_gates(e):
                    for i in range(1, RING):
                        load_unit(e, U_MG + i, i, std_parts("w_in", COL_MG)(0, i), U_MG + i - RING + 1)
                    weights(e, U_MG, U_OUT - U_MG, std_parts("w_in", COL_MG), lo=1)
                    weights(e, U_OUT, RING, out_parts)

                def gate_step(e, j, s):
                    tile_done_(e, U_MG + RING * j + s)
                    e.activation(halves(G[:, bass.ds(RING * j + s, 1), :].rearrange("p o t -> p (o t)")), out_tile(s % 2), ACT.Tanh,
                                 scale=0.5).then_inc(evac[s % 2], 1)

                def conv_step(e, j, s):
                    link = lambda i: dve_chain(e, i)
                    u = RING * j + s
                    for x in range(3 * u, min(3 * u + 3, 2 * CC)):
                        tap, c = x // 2, x % 2
                        w = vecs[:, V_CC + x:V_CC + x + 1]
                        for dst, src in ((y_c[:, c, 0:SEQ], u_c[:, c, tap:tap + SEQ]), (y_c[:, c, SEQ:], us_c[:, c, tap, :])):
                            if tap == 0:
                                link(e.tensor_scalar(dst, src, w, vecs[:, V_CB + c:V_CB + c + 1], ALU.mult, ALU.add))
                            else:
                                link(e.scalar_tensor_tensor(dst, src, w, dst, ALU.mult, ALU.add))

                stage_block(U_MG, U_OUT - U_MG, load_gates, gate_step, conv_step, unroll=True,
                            pe=lambda e: plain_stage(e, U_MG, U_OUT - U_MG, (act_hi, act_lo)))

                with nc.Block() as block:
                    @block.tensor
                    def _(e):
                        for h in range(2):
                            for c in range(2):
                                mm = e.matmul(pn[:, h, 0:HALF], ones[:], y_c[:, c, h * HALF:(h + 1) * HALF], start=c == 0, stop=c == 1)
                        mm.then_inc(mean_c, 1)
                        e.wait_ge(sqc, 1)
                        for tt in range(5):
                            w = P if tt < 4 else NB
                            for c in range(2):
                                mm = e.matmul(pa[0][0:w, tt:tt + 1], sq_c[:, c, tt * P:tt * P + w], ones[:, 0:1], start=c == 0, stop=c == 1)
                        mm.then_inc(var_c, 1)
                        e.wait_ge(dgcc, 1)
                        for h in range(2):
                            mm = e.matmul(pn[:, h, 0:HALF], ones[:], diag_c[:, h * HALF:(h + 1) * HALF], start=True, stop=True)
                        mm.then_inc(rbc, 1)

                    @block.gpsimd
                    def _(e):
                        e.wait_ge(msc, 1)
                        e.tensor_tensor(r_c[:], ms_c[:], minus_half[:], ALU.pow).then_inc(rc, 1)

                    @block.scalar
                    def _(e):
                        e.wait_ge(xc_ready, 1)
                        e.activation(sq_c[:], y_c[:], ACT.Square).then_inc(sqc, 1)
                        e.wait_ge(xn, 1)
                        for c in range(2):
                            mm = e.activation(y_c[:, c, :], y_c[:, c, :], ACT.Identity, bias=vecs[:, V_CS + c:V_CS + c + 1])
                        mm.then_inc(vc, 1)
                        e.wait_ge(vc, 1)
                        e.activation(sq_c[:], y_c[:], ACT.Tanh, scale=0.5).then_inc(thv, 1)

                    @block.vector
                    def _(e):
                        link = lambda i: dve_chain(e, i)
                        link(e.memset(ms_c[:], 1.0))
                        e.wait_ge(mean_c, 1)
                        for c in range(2):
                            mm = e.scalar_tensor_tensor(halves(y_c[:, c, :]), pn[:, :, 0:HALF], -1.0 / 256, halves(y_c[:, c, :]), ALU.mult, ALU.add)
                        mm.then_inc(xc_ready, 1)
                        e.wait_ge(var_c, 1)
                        link(e.tensor_scalar(ms_c[:, 0:4], pa[0][:, 0:4], 1.0 / 256, LN_EPS, ALU.mult, ALU.add))
                        e.tensor_scalar(ms_c[0:NB, 4:5], pa[0][0:NB, 4:5], 1.0 / 256, LN_EPS, ALU.mult, ALU.add).then_inc(msc, 1)
                        e.wait_ge(rc, 1)
                        link(e.tensor_tensor(diag_c[:, 0:SEQ].rearrange("p (t q) -> p t q", t=4),
                                             ident[:].rearrange("p (o q) -> p o q", o=1).broadcast_to([P, 4, P]),
                                             r_c[:, 0:4].rearrange("p (t o) -> p t o", o=1).broadcast_to([P, 4, P]), ALU.mult))
                        e.tensor_scalar(diag_c[:, SEQ:TOK], ident[:, 0:NB], r_c[:, 4:5], None, ALU.mult).then_inc(dgcc, 1)
                        e.wait_ge(rbc, 1)
                        e.wait_ge(xc_ready, 1)
                        for c in range(2):
                            mm = e.scalar_tensor_tensor(halves(y_c[:, c, :]), halves(y_c[:, c, :]), vecs[:, V_CG + c:V_CG + c + 1],
                                                        pn[:, :, 0:HALF], ALU.mult, ALU.mult)
                        mm.then_inc(xn, 1)
                        e.wait_ge(thv, 1)
                        link(e.scalar_tensor_tensor(y_c[:], sq_c[:], 1.0, y_c[:], ALU.add, ALU.mult))
                        e.tensor_scalar(sq_c[:], y_c[:], 0.5, None, ALU.mult)

                def load_out(e):
                    weights(e, U_OUT, U_WO - U_OUT, out_parts, lo=1)
                    weights(e, U_WO, RING, std_parts("w_o"))

                def three_products(e):
                    def group(j):
                        for s in range(RING):
                            m = RING * j + s
                            await_(e, w_ready, U_OUT + m + 1)
                            await_(e, evac[s % 2], U_OUT // 2 + 2 * j + s // 2)
                            for k in range(KC):
                                wk = slice(k * P, (k + 1) * P)
                                if k == 4:
                                    await_(e, merged, m)
                                first = k in (0, 4, 6)
                                for n, (w, x) in enumerate(((w_lo, act_hi), (w_hi, act_lo), (w_hi, act_hi))):
                                    for h in range(2):
                                        out = pg[:, s % 2, h, 0:HALF] if k < 4 else pn[:, h, 0:HALF] if k < 6 else pa[h][:, 0:HALF]
                                        mm = e.matmul(out, w[:, s % 2, wk], x[:, k, h * HALF:(h + 1) * HALF],
                                                      start=first and n == 0, stop=k in (3, 5, 7) and n == 2)
                            mm.then_inc(unit_done, 1)
                    group(0)
                    fori(e, 1, (U_WO - U_OUT) // RING, group)

                def merge_step(e, j, s):
                    link = lambda i: dve_chain(e, i)
                    m = RING * j + s
                    dve_chain.restart(e)
                    tile_done_(e, U_OUT + m)
                    g = [G[:, bass.ds(m + KC * i, 1), :].rearrange("p o t -> p (o t)") for i in range(3)]
                    e.scalar_tensor_tensor(halves(g[0]), halves(g[0]), 1.0, out_tile(s % 2), ALU.add, ALU.mult).then_inc(evac[s % 2], 1)
                    e.scalar_tensor_tensor(halves(g[1]), halves(g[1]), 1.0, pn[:, :, 0:HALF], ALU.add, ALU.mult)
                    for h in range(2):
                        mm = e.scalar_tensor_tensor(g[2][:, h * HALF:(h + 1) * HALF], g[2][:, h * HALF:(h + 1) * HALF], 1.0, pa[h][:, 0:HALF], ALU.add, ALU.mult)
                    mm.then_inc(merged, 1)
                    await_(e, merged, m + 1)
                    link(e.tensor_tensor(g[0], g[0], g[1], ALU.add))
                    link(e.tensor_tensor(g[0], g[0], g[2], ALU.add))

                stage_block(U_OUT, U_WO - U_OUT, load_out, lambda e, j, s: None, merge_step, source=lambda c: oac[:, c, :] if c < 6 else sq_c[:, c - 6, :], pe=three_products)
                Y = sb(scope, "Y", [P, KC, TOK])

                def load_wo(e):
                    weights(e, U_WO, U_XKV - U_WO, std_parts("w_o"), lo=1)
                    weights(e, U_XKV, RING, std_parts("w_xkv"))

                stage_block(U_WO, U_XKV - U_WO, load_wo, tile_to(Y, U_WO), source=lambda c: G[:, c, :], scale=0.5,
                            pe=lambda e: plain_stage(e, U_WO, U_XKV - U_WO, (act_hi, act_lo)))
                norm_block((1, Y, False), (2, xT, True))
            upto_b4.close()

            with phase_semaphores(), ExitStack() as scope:
                cmem = sb(scope, "cmem", [P, NB, 2, 2 * XH * XD])
                kvT = sb(scope, "kvT", [P, 2 * XH, N_MEM])
                qx = sb(scope, "qx", [P, XH, TOK])
                ox = sb(scope, "ox", [P, XH, TOK])
                mem_in, cm_in = sem("mem_in"), sem("cm_in")
                with ExitStack() as inner:
                    mem_f = sb(inner, "mem_f", [P, KC, N_MEM])
                    mem_hi = sb(inner, "mem_hi", [P, KC, N_MEM], F32R)
                    mem_lo = sb(inner, "mem_lo", [P, KC, N_MEM], F32R)
                    with nc.Block() as block:
                        @block.sync
                        def _(e):
                            e.dma_start(mem_f[:].rearrange("p c m -> p (c m)"), mem_dram.ap()).then_inc(mem_in, 16)

                        @block.vector
                        def _(e):
                            e.wait_ge(mem_in, 16)
                            for c in range(KC):
                                e.tensor_scalar(mem_f[:, c, :], mem_f[:, c, :], vecs[:, V_MEM + c:V_MEM + c + 1], None, ALU.mult)

                    def load_xkv(e):
                        weights(e, U_XKV, U_XQ - U_XKV, std_parts("w_xkv"), lo=1)
                        weights(e, U_XQ, RING, std_parts("w_xq"))
                        for b in range(NB):
                            e.dma_start(cmem[:, b], A["cache_mem"][bass.ds(L, 1), b:b + 1].rearrange("l o (t p) k h d -> p (l o t) (k h d)", p=P)
                                        ).then_inc(cm_in, 16)

                    stage_block(U_XKV, U_XQ - U_XKV, load_xkv, tile_to(kvT, U_XKV, N_MEM), source=lambda c: mem_f[:, c, :], operand=(mem_hi, mem_lo),
                                pe=lambda e: plain_stage(e, U_XKV, U_XQ - U_XKV, (mem_hi, mem_lo), widths=(N_MEM,)))
                stage_block(U_XQ, U_XO - U_XQ, lambda e: weights(e, U_XO, RING, xo_parts), tile_to(qx, U_XQ),
                            pe=lambda e: plain_stage(e, U_XQ, U_XO - U_XQ, (act_hi, act_lo)))

                with ExitStack() as inner:
                    mnat = sb(inner, "mnat", [P, 2, 2 * XH * XD])
                    px = sb(inner, "px", [P, 2, XH, N_MEM])
                    pxT = sb(inner, "pxT", [P, 2, 2, XH * P])
                    mxx = sb(inner, "mxx", [P, 2, XH])
                    dnx = sb(inner, "dnx", [P, 2, XH])
                    keyT = sb(inner, "keyT", [P, 2, XH * P])
                    lx = sb(inner, "lx", [P, 2, NB * XH])
                    mxc_ = sb(inner, "mxc_", [P, NB * XH])
                    topx = sb(inner, "topx", [NB * XH, 1])
                    dgx = sb(inner, "dgx", [NB * XH, NB * XH])
                    invx = sb(inner, "invx", [P, NB * XH])
                    XSCALE = XD ** -0.5
                    mn_tr, mn_cp, m_out, xl, xmx, xe, xp, xt, xtc, xpv, xo_s = (sem(n) for n in (
                        "mn_tr", "mn_cp", "m_out", "xl", "xmx", "xe", "xp", "xt", "xtc", "xpv", "xo_s"))
                    kt_tr, kt_cp, kt_mm, sx = (sem(n) for n in ("kt_tr", "kt_cp", "kt_mm", "sx"))
                    with nc.Block() as block:
                        @block.sync
                        def _(e):
                            e.wait_ge(mn_cp, 4)
                            e.dma_start(O["mem_kv_prompt"][bass.ds(L, 1)].rearrange("l o (t p) k h d -> p (l o t) (k h d)", p=P), mnat[:]).then_inc(m_out, 16)
                            e.wait_ge(m_out, 16)

                        @block.tensor
                        def _(e):
                            for n in range(4):
                                t, kv = n // 2, n % 2
                                if n >= 2:
                                    e.wait_ge(mn_cp, n - 1)
                                for h in range(XH):
                                    mm = e.transpose(pn[:, n % 2, h * P:(h + 1) * P], kvT[:, kv * XH + h, t * P:(t + 1) * P], ident[:])
                                mm.then_inc(mn_tr, 1)

                            def score(t):
                                if t >= 2:
                                    e.wait_ge(xe, t - 1)
                                for h in range(XH):
                                    mm = e.matmul(pg[:, t % 2, h // 2, (h % 2) * N_MEM:(h % 2 + 1) * N_MEM], qx[:, h, t * P:(t + 1) * P],
                                                  kvT[:, h, :], start=True, stop=True)
                                mm.then_inc(xl, 1)

                            def combine(t):
                                e.wait_ge(xp, t + 1)
                                e.wait_ge(mn_cp, 4)
                                if t:
                                    e.wait_ge(xtc, 2 * t)
                                for k in range(2):
                                    for h in range(XH):
                                        mm = e.transpose(pn[:, k, h * P:(h + 1) * P], px[:, t % 2, h, k * P:(k + 1) * P], ident[:])
                                mm.then_inc(xt, 1)
                                e.wait_ge(xtc, 2 * t + 2)
                                if t >= 2:
                                    e.wait_ge(xo_s, t - 1)
                                for h in range(XH):
                                    for k in range(2):
                                        mm = e.matmul(pa[t % 2][:, h * P:(h + 1) * P], mnat[:, k, (XH + h) * XD:(XH + h + 1) * XD],
                                                      pxT[:, t % 2, k, h * P:(h + 1) * P], start=k == 0, stop=k == 1)
                                mm.then_inc(xpv, 1)
                            score(0)
                            for t in range(QT):
                                if t + 1 < QT:
                                    score(t + 1)
                                combine(t)
                            e.wait_ge(cm_in, 16 * NB)
                            e.wait_ge(xtc, 2 * QT)
                            e.wait_ge(xe, QT)
                            N = 2 * NB
                            for n in range(N + 1):
                                if n < N:
                                    b, t = n // 2, n % 2
                                    if n >= 2:
                                        e.wait_ge(kt_cp, n - 1)
                                    for h in range(XH):
                                        mm = e.transpose(pn[:, n % 2, h * P:(h + 1) * P], cmem[:, b, t, h * XD:(h + 1) * XD], ident[:])
                                    mm.then_inc(kt_tr, 1)
                                if n >= 1:
                                    b, t = (n - 1) // 2, (n - 1) % 2
                                    e.wait_ge(kt_cp, n)
                                    for h in range(XH):
                                        mm = e.matmul(pg[:, 0, 0, t * 32 + b * XH + h:t * 32 + b * XH + h + 1], keyT[:, (n - 1) % 2, h * P:(h + 1) * P],
                                                      qx[:, h, SEQ + b:SEQ + b + 1], start=True, stop=True)
                                    mm.then_inc(kt_mm, 1)
                            e.wait_ge(sx, 1)
                            e.transpose(pg[0:NB * XH, 0, 1, 0:P], mxc_[:], ident[:]).then_inc(sx, 1)
                            e.wait_ge(sx, 3)
                            e.matmul(pg[:, 1, 0, 0:32], ones[0:32, :], dgx[:], start=True, stop=True).then_inc(sx, 1)
                            e.wait_ge(sx, 6)
                            for t in range(2):
                                mm = e.matmul(pg[:, 1, 0, 32:64], ones[:], lx[:, t, :], start=t == 0, stop=t == 1)
                            for b in range(NB):
                                for h in range(XH):
                                    for t in range(2):
                                        mm = e.matmul(pg[:, 1, 1, b * XH + h:b * XH + h + 1], cmem[:, b, t, (XH + h) * XD:(XH + h + 1) * XD],
                                                      lx[:, t, b * XH + h:b * XH + h + 1], start=t == 0, stop=t == 1)
                            mm.then_inc(sx, 1)

                        @block.scalar
                        def _(e):
                            for t in range(QT + 1):
                                if t < QT:
                                    e.wait_ge(xmx, t + 1)
                                    if t >= 2:
                                        e.wait_ge(xt, t - 1)
                                    for h in range(XH):
                                        mm = e.activation(px[:, t % 2, h, :], pg[:, t % 2, h // 2, (h % 2) * N_MEM:(h % 2 + 1) * N_MEM], ACT.Exp,
                                                          scale=XSCALE, bias=mxx[:, t % 2, h:h + 1], accum_out=dnx[:, t % 2, h:h + 1])
                                    mm.then_inc(xe, 1)
                                if t >= 1:
                                    u = t - 1
                                    e.wait_ge(xt, u + 1)
                                    if u >= 2:
                                        e.wait_ge(xpv, u - 1)
                                    e.copy(pxT[:, u % 2, 0, :], pn[:, 0, :]).then_inc(xtc, 1)
                            for n in range(0, 2 * NB, 2):
                                e.wait_ge(kt_tr, n + 1)
                                if n >= 2:
                                    e.wait_ge(kt_mm, n - 1)
                                    e.wait_ge(kt_cp, n)
                                e.copy(keyT[:, 0, :], pn[:, 0, :]).then_inc(kt_cp, 1)
                            e.wait_ge(sx, 5)
                            e.activation(lx[:], lx[:], ACT.Exp, scale=XSCALE).then_inc(sx, 1)

                        @block.vector
                        def _(e):
                            link = lambda i: dve_chain(e, i)
                            for n in range(4):
                                e.wait_ge(mn_tr, n + 1)
                                e.tensor_copy(mnat[:, n // 2, (n % 2) * 512:(n % 2 + 1) * 512], pn[:, n % 2, :]).then_inc(mn_cp, 1)
                            for t in range(QT + 1):
                                if t < QT:
                                    e.wait_ge(xl, t + 1)
                                    link(e.tensor_reduce(mxx[:, t % 2, :], pg[:, t % 2].rearrange("p a (b m) -> p (a b) m", m=N_MEM), AX.X, ALU.max))
                                    e.tensor_scalar(mxx[:, t % 2, :], mxx[:, t % 2, :], -XSCALE, None, ALU.mult).then_inc(xmx, 1)
                                if t >= 1:
                                    u = t - 1
                                    e.wait_ge(xe, u + 1)
                                    link(e.reciprocal(dnx[:, u % 2, :], dnx[:, u % 2, :]))
                                    e.tensor_tensor(px[:, u % 2], px[:, u % 2], dnx[:, u % 2, :].rearrange("p (h o) -> p h o", o=1).broadcast_to([P, XH, N_MEM]),
                                                    ALU.mult).then_inc(xp, 1)
                                    e.wait_ge(xt, u + 1)
                                    e.wait_ge(xtc, 2 * u + 1)
                                    e.tensor_copy(pxT[:, u % 2, 1, :], pn[:, 1, :]).then_inc(xtc, 1)
                                    e.wait_ge(xpv, u + 1)
                                    e.tensor_copy(ox[:, :, u * P:(u + 1) * P], pa[u % 2][:].rearrange("p (h q) -> p h q", h=XH)).then_inc(xo_s, 1)
                            for n in range(1, 2 * NB, 2):
                                e.wait_ge(kt_tr, n + 1)
                                e.wait_ge(kt_cp, n)
                                if n >= 2:
                                    e.wait_ge(kt_mm, n - 1)
                                e.tensor_copy(keyT[:, 1, :], pn[:, 1, :]).then_inc(kt_cp, 1)
                            e.wait_ge(kt_mm, 2 * NB)
                            link(e.tensor_copy(lx[:].rearrange("p t x -> p (t x)"), pg[:, 0, 0, 0:64]))
                            e.tensor_tensor(mxc_[:], lx[:, 0, :], lx[:, 1, :], ALU.max).then_inc(sx, 1)
                            e.wait_ge(sx, 2)
                            link(e.tensor_reduce(topx[:], pg[0:NB * XH, 0, 1, 0:P], AX.X, ALU.max))
                            e.tensor_scalar(dgx[:], ident[0:32, 0:32], topx[:, 0:1], None, ALU.mult).then_inc(sx, 1)
                            e.wait_ge(sx, 4)
                            e.tensor_tensor(lx[:], lx[:], pg[:, 1, 0:1, 0:32].broadcast_to([P, 2, 32]), ALU.subtract).then_inc(sx, 1)
                            e.wait_ge(sx, 7)
                            link(e.reciprocal(invx[:], pg[:, 1, 0, 32:64]))
                            e.tensor_tensor(ox[:, :, SEQ:].rearrange("p h b -> p b h"), pg[:, 1, 1, 0:32].rearrange("p (b h) -> p b h", h=XH),
                                            invx[:].rearrange("p (b h) -> p b h", h=XH), ALU.mult)

                Y = sb(scope, "Yx", [P, KC, TOK])

                def load_xo(e):
                    weights(e, U_XO, U_FI - U_XO, xo_parts, lo=1)
                    weights(e, U_FI, RING, fi_parts)

                stage_block(U_XO, U_FI - U_XO, load_xo, tile_to(Y, U_XO), source=lambda c: ox[:, c, :], chunks=XH,
                            pe=lambda e: plain_stage(e, U_XO, U_FI - U_XO, (act_hi, act_lo), kn=XH))
                norm_block((3, Y, False), (4, xT, True))

            def fo_load(e, m, i):
                r0, kn = 1024 * i, KC if i < 2 else FC - 2 * KC
                load_unit(e, U_FO + 3 * m + i, (3 * m + i) % RING,
                          [(slot_view((3 * m + i) % RING)[:, 0:kn, :], cols("w_ffn_out", P * m, slice(r0, r0 + kn * P)))],
                          U_FO + 3 * m + i - RING + 1)

            with ExitStack() as scope:
                hid_hi = sb(scope, "hid_hi", [P, FC, TOK], F32R)
                hid_lo = sb(scope, "hid_lo", [P, FC, TOK], F32R)
                th_f, hf = sem("th_f"), sem("hf")
                with ExitStack() as inner:
                    thf = sb(inner, "thf", [P, 2, TOK])
                    t1 = sb(inner, "silu2", [P, 2, TOK])
                    t2 = sb(inner, "hid_f", [P, 2, TOK])

                    def load_fi(e):
                        weights(e, U_FI, U_FO - U_FI, fi_parts, lo=1)
                        for n in range(RING):
                            fo_load(e, n // 3, n % 3)

                    def fi_act(e, j, s):
                        f = 2 * j + s // 2
                        if s % 2 == 0:
                            tile_done_(e, U_FI + RING * j + s)
                            e.activation(halves(thf[:, s // 2, :]), out_tile(0), ACT.Tanh, scale=0.5).then_inc(th_f, 1)
                        else:
                            await_(e, evac[1], U_FI // 2 + f + 1)
                            e.copy(hid_hi[:, bass.ds(f, 1), :].rearrange("p o t -> p (o t)"), t2[:, s // 2, :]).then_inc(hf, 1)

                    def fi_dve(e, j, s):
                        f = 2 * j + s // 2
                        if s % 2 == 0:
                            await_(e, th_f, f + 1)
                            e.scalar_tensor_tensor(halves(t1[:, s // 2, :]), halves(thf[:, s // 2, :]), 1.0, out_tile(0), ALU.add, ALU.mult
                                                   ).then_inc(evac[0], 1)
                        else:
                            tile_done_(e, U_FI + RING * j + s)
                            await_(e, evac[0], U_FI // 2 + f + 1)
                            e.scalar_tensor_tensor(halves(t2[:, s // 2, :]), halves(t1[:, s // 2, :]), 0.5, out_tile(1), ALU.mult, ALU.mult
                                                   ).then_inc(evac[1], 1)
                            await_(e, hf, f + 1)
                            hi = hid_hi[:, bass.ds(f, 1), :].rearrange("p o t -> p (o t)").bitcast(F32)
                            e.tensor_tensor(hid_lo[:, bass.ds(f, 1), :].rearrange("p o t -> p (o t)"), t2[:, s // 2, :], hi, ALU.subtract)

                    stage_block(U_FI, U_FO - U_FI, load_fi, fi_act, fi_dve,
                                pe=lambda e: plain_stage(e, U_FI, U_FO - U_FI, (act_hi, act_lo)))
                Y = sb(scope, "Yf", [P, KC, TOK])

                def load_fo(e):
                    for n in range(RING, 3 * KC):
                        fo_load(e, n // 3, n % 3)

                def thirds(e, split, step):
                    for n in range(3 * KC):
                        v = U_FO + n + 1
                        if v < U_END:
                            split(v, v % RING, landed(v))
                        if n % 3 == 2:
                            step(n // 3)

                def fo_act(e, m):
                    tile_done_(e, U_FO + 3 * m + 2)
                    e.copy(halves(Y[:, m, :]), out_tile(m % 2)).then_inc(evac[m % 2], 1)

                def fo_pe(e):
                    def body(j):
                        for n in range(12):
                            m, i = n // 3, n % 3
                            products(e, U_FO + 12 * j + n, n % RING, U_FO // 2 + 2 * j + m // 2, m % 2, KC * i, KC if i < 2 else FC - 2 * KC,
                                     (hid_hi, hid_lo), i == 0, i == 2, (HALF, HALF))
                    fori(e, 0, 2, body)

                stage_block(U_FO, 3 * KC, load_fo, fo_act, pe=fo_pe, last=thirds)
                norm_block((5, Y, False))

            semaphores_to_zero()

        with ExitStack() as scope:
            rows_out = sb(scope, "rows_out", [P, 5, D_MODEL])
            y_tr, y_cp, y_out = sem("y_tr"), sem("y_cp"), sem("y_out")
            with nc.Block() as block:
                @block.tensor
                def _(e):
                    for n in range(10):
                        t, q = n // 2, n % 2
                        w = P if t < QT else NB
                        if n >= 2:
                            e.wait_ge(y_cp, n - 1)
                        for c in range(4):
                            mm = e.transpose(pa[n % 2][0:w, c * P:(c + 1) * P], xT[:, 4 * q + c, t * P:t * P + w], ident[:])
                        mm.then_inc(y_tr, 1)

                @block.vector
                def _(e):
                    for n in range(10):
                        t, q = n // 2, n % 2
                        w = P if t < QT else NB
                        e.wait_ge(y_tr, n + 1)
                        e.tensor_copy(rows_out[0:w, t, q * 512:(q + 1) * 512], pa[n % 2][0:w, :]).then_inc(y_cp, 1)

                @block.sync
                def _(e):
                    for t in range(QT):
                        e.wait_ge(y_cp, 2 * t + 2)
                        e.dma_start(O["y_prompt"].rearrange("o (t p) d -> t p (o d)", p=P)[t], rows_out[:, t, :]).then_inc(y_out, 16)
                    e.wait_ge(y_cp, 10)
                    e.dma_start(O["y_sample"].rearrange("b o d -> (b o) d"), rows_out[0:NB, QT, :]).then_inc(y_out, 16)
                    e.wait_ge(y_out, 16 * (QT + 1))


INS = ["x_prompt", "x_sample", "mem_prompt", "cache_kv", "page_table", "cache_win", "state_conv_a", "state_conv_c",
       "cache_mem", "rel_bias", "norm_g", "mem_norm_g", "w_in", "conv_a_w", "conv_c_w", "conv_c_b", "conv_c_ln_g",
       "conv_c_ln_b", "cmp_w1", "cmp_b1", "cmp_w2", "cmp_b2", "cmp_pe", "w_nsa_out", "w_a_out", "w_c_out", "w_o",
       "w_xq", "w_xkv", "w_xo", "w_ffn_in", "w_ffn_out"]
OUTS = [("y_prompt", (1, SEQ, D_MODEL)), ("y_sample", (NB, 1, D_MODEL)),
        ("kv_prompt", (DEPTH, 1, SEQ, 4, N_KV, HD)), ("kv_sample", (DEPTH, NB, 1, 4, N_KV, HD)),
        ("win_prompt", (DEPTH, 1, WINDOW, 2, N_KV, HD)), ("win_sample", (DEPTH, NB, WINDOW, 2, N_KV, HD)),
        ("conv_a_prompt", (DEPTH, 1, CA - 1, 256)), ("conv_a_sample", (DEPTH, NB, CA - 1, 256)),
        ("conv_c_prompt", (DEPTH, 1, CC - 1, 256)), ("conv_c_sample", (DEPTH, NB, CC - 1, 256)),
        ("mem_kv_prompt", (DEPTH, 1, N_MEM, 2, XH, XD))]


def kernel(**inputs):
    import concourse.bacc as bacc
    from concourse.bass_utils import run_bass_kernel_spmd

    nc = bacc.Bacc("TRN2", target_bir_lowering=False, num_devices=1)
    arrays, ins, outs = {}, {}, {}
    for name in INS:
        a = np.ascontiguousarray(inputs[name])
        arrays["in_" + name] = a
        ins[name] = nc.dram_tensor("in_" + name, a.shape, mybir.dt.from_np(a.dtype), kind="ExternalInput").ap()
    for name, shape in OUTS:
        outs[name] = nc.dram_tensor("out_" + name, shape, F32, kind="ExternalOutput").ap()
    build(nc, ins, outs)
    r = run_bass_kernel_spmd(nc, [arrays], core_ids=[0])
    return tuple(r.results[0]["out_" + name] for name, _ in OUTS)
```
